# Optimizing a Trainium2 kernel written in Bass

```python
import math
import jax, jax.numpy as jnp
from jax import lax
import numpy as np

D_MODEL = 1024
BATCH = 1
SEQ = 1024
DEPTH = 2
DEC_BATCH = 8
DEC_SEQ = 8
PAST_LEN = 4096
PAGE_SIZE = 128

N_A_LAYERS = DEPTH // 2
N_B_LAYERS = DEPTH - N_A_LAYERS
POOL_WINDOWS = (2, 4, 8, 16)
N_POOL_GROUPS = len(POOL_WINDOWS)
POOL_GROUP_DIM = D_MODEL // N_POOL_GROUPS
POOL_HIST = max(POOL_WINDOWS) - 1
HEAD_DIM = 64
N_HEADS = D_MODEL // HEAD_DIM
D_FF = 4 * D_MODEL
Q_BLOCK = 128
LN_EPS = 1e-5
DN_ALPHA = float((2 * DEPTH) ** 0.25)
DN_BETA = float((8 * DEPTH) ** -0.25)
BREAK_BIAS_LO = 4.0
BREAK_BIAS_HI = 9.0

kernel_name = "yoco_pool_stickbreak_decoder_step"

def _layer_norm(x, g, b):
    xf = x.astype(jnp.float32)
    mu = jnp.mean(xf, axis=-1, keepdims=True)
    var = jnp.mean(jnp.square(xf - mu), axis=-1, keepdims=True)
    y = (xf - mu) * lax.rsqrt(var + LN_EPS) * g.astype(jnp.float32) + b.astype(jnp.float32)
    return y.astype(x.dtype)

def _ada(c, w, b):
    m = jax.nn.silu(c) @ w + b
    return [t[:, None, :] for t in jnp.split(m, 6, axis=-1)]

def _pool_mixer(h, hist, pos0, w_pool, pool_scale):
    T = h.shape[1]
    ext = jnp.concatenate([hist, h], axis=1)
    extf = ext.astype(jnp.float32)
    cs = jnp.cumsum(extf, axis=1)
    cs0 = jnp.concatenate([jnp.zeros_like(cs[:, :1]), cs], axis=1)
    pos = pos0 + jnp.arange(T)
    outs = []
    for g, w in enumerate(POOL_WINDOWS):
        sl = slice(g * POOL_GROUP_DIM, (g + 1) * POOL_GROUP_DIM)
        hi = cs0[:, POOL_HIST + 1:POOL_HIST + 1 + T, sl]
        lo = cs0[:, POOL_HIST + 1 - w:POOL_HIST + 1 - w + T, sl]
        cnt = jnp.minimum(w, pos + 1).astype(jnp.float32)[None, :, None]
        d = ((hi - lo) / cnt - extf[:, POOL_HIST:, sl]).astype(h.dtype)
        outs.append(d @ w_pool[g])
    out = jnp.concatenate(outs, axis=-1) * pool_scale
    return out, ext[:, -POOL_HIST:]

def _stick_breaking(q, k, v, q_pos0, break_bias):
    T = q.shape[1]
    L = k.shape[1]
    blk = min(Q_BLOCK, T)
    scale = HEAD_DIM ** -0.5
    bias = break_bias.astype(jnp.float32)[None, :, None, None]
    outs = []
    for start in range(0, T, blk):
        qb = q[:, start:start + blk]
        nb = qb.shape[1]
        kv_len = min(L, q_pos0 + start + nb)
        kb = k[:, :kv_len]
        vb = v[:, :kv_len]
        z = jnp.einsum('bqhd,bkhd->bhqk', qb, kb, preferred_element_type=jnp.float32) * scale + bias
        qpos = q_pos0 + start + jnp.arange(nb)
        kpos = jnp.arange(kv_len)
        mask = kpos[None, :] < qpos[:, None]
        log_beta = jax.nn.log_sigmoid(z)
        log_keep = jnp.where(mask, log_beta - z, 0.0)
        rest = lax.cumsum(log_keep, axis=3, reverse=True) - log_keep
        a = jnp.where(mask, jnp.exp(log_beta + rest), 0.0)
        outs.append(jnp.einsum('bhqk,bkhd->bqhd', a.astype(vb.dtype), vb))
    return jnp.concatenate(outs, axis=1)

def setup_inputs(seed: int = 0) -> dict:
    key = jax.random.key(seed)
    ks = jax.random.split(key, 20)
    n_pages = PAST_LEN // PAGE_SIZE
    n_used = DEC_BATCH * n_pages
    n_pool_pages = n_used + max(1, n_used // 4)
    f32 = jnp.float32
    x_prompt = jax.random.normal(ks[0], (BATCH, SEQ, D_MODEL), f32)
    x_sample = jax.random.normal(ks[1], (DEC_BATCH, DEC_SEQ, D_MODEL), f32)
    cache_k = jax.random.normal(ks[2], (n_pool_pages, PAGE_SIZE, N_HEADS, HEAD_DIM), f32)
    cache_v = jax.random.normal(ks[3], (n_pool_pages, PAGE_SIZE, N_HEADS, HEAD_DIM), f32) * DN_BETA
    state_pool = jax.random.normal(ks[4], (N_A_LAYERS, DEC_BATCH, POOL_HIST, D_MODEL), f32)
    page_table = jax.random.permutation(ks[5], n_pool_pages)[:n_used].reshape(DEC_BATCH, n_pages).astype(jnp.int32)
    c_prompt = jax.random.normal(ks[6], (BATCH, D_MODEL), f32)
    c_sample = jax.random.normal(ks[7], (DEC_BATCH, D_MODEL), f32)
    w_ada = jax.random.normal(ks[8], (DEPTH, D_MODEL, 6 * D_MODEL), f32) * (0.5 * D_MODEL ** -0.5)
    b_ada = jax.random.normal(ks[9], (DEPTH, 6 * D_MODEL), f32) * 0.02
    ln_g = 1.0 + 0.05 * jax.random.normal(ks[10], (DEPTH, 2, D_MODEL), f32)
    ln_b = 0.02 * jax.random.normal(ks[11], (DEPTH, 2, D_MODEL), f32)
    w_pool = jax.random.normal(ks[12], (N_A_LAYERS, N_POOL_GROUPS, POOL_GROUP_DIM, POOL_GROUP_DIM), f32) * (POOL_GROUP_DIM ** -0.5 * DN_BETA)
    pool_scale = 1.0 + 0.1 * jax.random.normal(ks[13], (N_A_LAYERS, D_MODEL), f32)
    w_up = jax.random.normal(ks[14], (DEPTH, D_MODEL, D_FF), f32) * D_MODEL ** -0.5
    w_down = jax.random.normal(ks[15], (DEPTH, D_FF, D_MODEL), f32) * (D_FF ** -0.5 * DN_BETA)
    kv_scale = jnp.concatenate([jnp.ones((D_MODEL,), f32), jnp.full((D_MODEL,), DN_BETA, f32)])
    w_kv = jax.random.normal(ks[16], (D_MODEL, 2 * D_MODEL), f32) * D_MODEL ** -0.5 * kv_scale
    w_q = jax.random.normal(ks[17], (N_B_LAYERS, D_MODEL, D_MODEL), f32) * D_MODEL ** -0.5
    w_o = jax.random.normal(ks[18], (N_B_LAYERS, D_MODEL, D_MODEL), f32) * (D_MODEL ** -0.5 * DN_BETA)
    b_break = (-jnp.linspace(BREAK_BIAS_LO, BREAK_BIAS_HI, N_HEADS, dtype=f32)[None, :]
               + 0.1 * jax.random.normal(ks[19], (N_B_LAYERS, N_HEADS), f32))
    return {"x_prompt": x_prompt, "x_sample": x_sample, "cache_k": cache_k, "cache_v": cache_v,
            "state_pool": state_pool, "page_table": page_table, "c_prompt": c_prompt, "c_sample": c_sample,
            "w_ada": w_ada, "b_ada": b_ada, "ln_g": ln_g, "ln_b": ln_b, "w_pool": w_pool,
            "pool_scale": pool_scale, "w_up": w_up, "w_down": w_down, "w_kv": w_kv, "w_q": w_q, "w_o": w_o,
            "b_break": b_break}

def reference(x_prompt, x_sample, cache_k, cache_v, state_pool, page_table, c_prompt, c_sample,
              w_ada, b_ada, ln_g, ln_b, w_pool, pool_scale, w_up, w_down, w_kv, w_q, w_o, b_break):
    def run_group(x, c, pool_hist, pos0, past_k, past_v):
        bsz, T, _ = x.shape
        new_hist = []
        keys = vals = k_new = v_new = None
        for layer in range(DEPTH):
            sh1, sc1, g1, sh2, sc2, g2 = _ada(c, w_ada[layer], b_ada[layer])
            if layer == N_A_LAYERS:
                kv = x @ w_kv
                k_new = kv[..., :D_MODEL].reshape(bsz, T, N_HEADS, HEAD_DIM)
                v_new = kv[..., D_MODEL:].reshape(bsz, T, N_HEADS, HEAD_DIM)
                if past_k is None:
                    keys, vals = k_new, v_new
                else:
                    keys = jnp.concatenate([past_k, k_new], axis=1)
                    vals = jnp.concatenate([past_v, v_new], axis=1)
            h = x * (1.0 + sc1) + sh1
            if layer < N_A_LAYERS:
                mix, hist = _pool_mixer(h, pool_hist[layer], pos0, w_pool[layer], pool_scale[layer])
                new_hist.append(hist)
            else:
                j = layer - N_A_LAYERS
                q = (h @ w_q[j]).reshape(bsz, T, N_HEADS, HEAD_DIM)
                o = _stick_breaking(q, keys, vals, pos0, b_break[j])
                mix = o.reshape(bsz, T, D_MODEL) @ w_o[j]
            x = _layer_norm(DN_ALPHA * x + g1 * mix, ln_g[layer, 0], ln_b[layer, 0])
            h = x * (1.0 + sc2) + sh2
            f = jnp.square(jax.nn.relu(h @ w_up[layer])) @ w_down[layer]
            x = _layer_norm(DN_ALPHA * x + g2 * f, ln_g[layer, 1], ln_b[layer, 1])
        return x, jnp.stack(new_hist, axis=0), k_new, v_new

    zero_hist = jnp.zeros((N_A_LAYERS, x_prompt.shape[0], POOL_HIST, D_MODEL), x_prompt.dtype)
    y_prompt, pool_prompt, k_prompt, v_prompt = run_group(x_prompt, c_prompt, zero_hist, 0, None, None)

    dec_b, n_pages = page_table.shape
    past_len = n_pages * PAGE_SIZE
    past_k = cache_k[page_table].reshape(dec_b, past_len, N_HEADS, HEAD_DIM)
    past_v = cache_v[page_table].reshape(dec_b, past_len, N_HEADS, HEAD_DIM)
    y_sample, pool_sample, k_sample, v_sample = run_group(x_sample, c_sample, state_pool, past_len, past_k, past_v)

    return (y_prompt, y_sample, k_prompt, v_prompt, pool_prompt, k_sample, v_sample, pool_sample)


_drawn_inputs = setup_inputs


def setup_inputs(seed=0):
    import zlib

    import numpy as np

    out = dict(_drawn_inputs(seed))
    spreads = {}
    factors = {'cache_k': 8.0, 'cache_v': 8.0, 'pool_scale': 5.61, 'w_q': 8.0, 'w_o': 8.0, 'b_break': 8.0}
    for name, (base, spread) in spreads.items():
        noise = np.random.default_rng([zlib.crc32(name.encode()), seed]).standard_normal(out[name].shape)
        drawn = base * np.exp(spread * noise) if base else spread * noise
        out[name] = __import__('jax').numpy.asarray(drawn.astype(out[name].dtype))
    for name, factor in factors.items():
        out[name] = (out[name] * factor).astype(out[name].dtype)
    return out
```

```python
from contextlib import ExitStack

import concourse.bass as bass
from concourse import mybir

ALU = mybir.AluOpType
ACT = mybir.ActivationFunctionType
AX = mybir.AxisListType
F32, F32R, BF16, I32 = mybir.dt.float32, mybir.dt.float32r, mybir.dt.bfloat16, mybir.dt.int32

P = 128
D = 1024
NC = D // P
TP = 1024
DB, DS = 8, 8
TS = DB * DS
T = TP + TS
WIN = (2, 4, 8, 16)
HIST = 15
H, HD = 16, 64
DFF = 4096
PAGES = 32
PIECES = [(0, 364), (364, 364), (728, 360)]
LASTP = TP - 728
ALPHA = 4.0 ** 0.25
EPS = 1e-5 / ALPHA ** 2
MASKED = -1e30


class Kernel:
    pass


def sems(ctx, nc, phase, *names):
    got = [nc.alloc_semaphore(f"{phase}_{n}") for n in names]
    ctx.callback(retire, nc, got)
    return got


def retire(nc, got):
    nc.clear_and_free_semaphores(got)
    nc.all_engine_barrier()


class Tally:

    def __init__(self, eng, sem):
        self.eng, self.sem, self.base, self.k = eng, sem, 0, 0

    def mark(self, ins):
        ins.then_inc(self.sem, 1)
        self.k += 1

    def settle(self):
        if isinstance(self.base, int) and self.base + self.k == 0:
            return
        self.eng.wait_ge(self.sem, self.base + self.k)

    def do(self, ins):
        self.mark(ins)
        self.settle()


def over(ap, n):
    return ap.unsqueeze(len(ap.shape)).to_broadcast(list(ap.shape) + [n])


def three(pe, out, w_hi, w_lo, x_hi, x_lo, start, stop):
    pe.matmul(out, w_hi, x_hi, start=start, stop=False, skip_group_check=True)
    pe.matmul(out, w_hi, x_lo, start=False, stop=False, skip_group_check=True)
    return pe.matmul(out, w_lo, x_hi, start=False, stop=stop, skip_group_check=True)


def setup(nc, k, a):
    with ExitStack() as ctx:
        at = k.at
        x_rows = at("x_rows", [P, 9, D], F32, k.HH_AT)
        c_rows = at("c_rows", [P, D], F32, k.F_AT)
        c_e = at("c_e", [P, D], F32, k.F_AT + 4096)
        vec_rows = at("vec_rows", [P, 2, P], F32, k.F_AT + 8192)
        c_t = at("c_t", [P, NC, 32], F32, k.F_AT + 9216)
        mod_rows = at("mod_rows", [P, 2, 512], F32, k.F_AT + 10240)
        w_raw = at("w_raw", [P, 4, 2048], F32, k.WORK_AT)
        ps = k.ps
        (x_in, c_in, v_in, made, x_turned, x_kept, x_free, c_done, c_turned, act_own, dve_own,
         ada_used, mod_kept, mod_turned, mod_out, v_turned, v_kept, b_in, z_set) = sems(
            ctx, nc, "set", "x_in", "c_in", "v_in", "made", "x_turned", "x_kept", "x_free", "c_done", "c_turned",
            "act_own", "dve_own", "ada_used", "mod_kept", "mod_turned", "mod_out", "v_turned",
            "v_kept", "b_in", "z_set")
        w_in = sems(ctx, nc, "set", "w_in0", "w_in1", "w_in2", "w_in3")
        block = ctx.enter_context(nc.Block())
        XJOBS = 18
        NIT = 3

        @block.sync
        def _(sp):
            sp.wait_ge(z_set, 2)
            sp.dma_start(c_rows[0:1, :], a["c_prompt"]).then_inc(c_in, 16)
            sp.dma_start(c_rows[1:9, :], a["c_sample"]).then_inc(c_in, 16)
            sp.dma_start(vec_rows[0:96, 0, :], a["b_ada"].rearrange("l (m p) -> (l m) p", p=P)).then_inc(v_in, 16)
            sp.dma_start(vec_rows[0:32, 1, :], a["ln_g"].rearrange("l s (m p) -> (l s m) p", p=P)).then_inc(v_in, 16)
            sp.dma_start(vec_rows[32:64, 1, :], a["ln_b"].rearrange("l s (m p) -> (l s m) p", p=P)).then_inc(v_in, 16)
            sp.dma_start(vec_rows[64:72, 1, :], a["pool_scale"].rearrange("l (m p) -> (l m) p", p=P)).then_inc(v_in, 16)
            sp.dma_start(k.bias_all[:, :], a["b_break"][0].partition_broadcast(P)).then_inc(b_in, 16)
            sp.dma_start(k.pages[:, :], a["page_table"].rearrange("b n -> (b n)").unsqueeze(0)).then_inc(b_in, 16)
            sp.dma_start(x_rows[:, 0:8, :], a["x_prompt"][0].rearrange("(t p) d -> p t d", p=P)).then_inc(x_in, 16)
            sp.dma_start(x_rows[0:TS, 8, :], a["x_sample"].rearrange("b t d -> (b t) d")).then_inc(x_in, 16)
            for layer in range(2):
                w = a["w_ada"][layer].rearrange("(k p) n -> k p n", p=P)
                with sp.Fori(0, NIT) as it:
                    for c in range(NC):
                        n = it * NC + (layer * NIT * NC + c)
                        sp.wait_ge(ada_used, n + 1)
                        sp.dma_start(w_raw[:, c % 4, :], w[c, :, bass.ds(it * 2048, 2048)]).then_inc(w_in[c % 4], 16)
            sp.wait_ge(b_in, 32)

        @block.gpsimd
        def _(pool):
            def made_by(ins):
                ins.then_inc(made, 1)
                made_by.n += 1
                pool.wait_ge(made, made_by.n)
            made_by.n = 0
            pool.memset(c_rows[:, :], 0.0).then_inc(z_set, 1)
            pool.memset(vec_rows[:, :, :], 0.0).then_inc(z_set, 1)
            made_by(pool.memset(k.ident[:, :], 0.0))
            made_by(pool.affine_select(out=k.ident[:, :], in_=k.ident[:, :], compare_op=ALU.not_equal, fill=1.0,
                                       base=0, pattern=[[-1, P]], channel_multiplier=1))
            made_by(pool.memset(k.mean_of[:, :], 1.0 / D))
            made_by(pool.memset(k.neg_ones[:, :], -1.0))
            made_by(pool.memset(k.neg_tri[:, :], -1.0))
            made_by(pool.affine_select(out=k.neg_tri[:, :], in_=k.neg_tri[:, :], compare_op=ALU.is_ge, fill=0.0,
                                       base=0, pattern=[[-1, P]], channel_multiplier=1))
            made_by(pool.memset(k.scratch[:, :], 0.0))
            made_by(pool.affine_select(out=k.scratch[:, :], in_=k.scratch[:, :], compare_op=ALU.is_gt, fill=MASKED,
                                       base=0, pattern=[[1, P]], channel_multiplier=-1))
            made_by(pool.tensor_copy(k.mask_diag[:, :], k.scratch[:, :]))
            made_by(pool.memset(k.scratch[:, :], 0.0))
            s3 = k.scratch[:, :].rearrange("p (h q) -> p h q", q=DS)
            made_by(pool.affine_select(out=s3, in_=s3, compare_op=ALU.is_gt, fill=MASKED, base=0,
                                       pattern=[[0, H], [1, DS]], channel_multiplier=-1))
            made_by(pool.tensor_copy(k.mask_new[:, :], k.scratch[:, :]))
            made_by(pool.tensor_copy(k.ident_b[:, :], k.ident[:, :]))
            made_by(pool.memset(k.head_of[:, :], 1.0))
            made_by(pool.affine_select(out=k.head_of[:, :], in_=k.head_of[:, :], compare_op=ALU.is_ge, fill=0.0,
                                       base=0, pattern=[[-DS, H]], channel_multiplier=1))
            made_by(pool.affine_select(out=k.head_of[:, :], in_=k.head_of[:, :], compare_op=ALU.is_ge, fill=0.0,
                                       base=DS - 1, pattern=[[DS, H]], channel_multiplier=-1))
            for t in range(HIST):
                made_by(pool.memset(k.inv_seen[:, t:t + 1], 1.0 / (t + 1)))

        MADE = 16 + HIST

        @block.scalar
        def _(act):
            own = Tally(act, act_own)
            act.wait_ge(c_in, 32)
            own.mark(act.activation(c_e[:, :], c_rows[:, :], ACT.Exp, scale=-1.0))
            for j in range(1, XJOBS, 2):
                t, half = j // 2, j % 2
                rows = P if t < 8 else TS
                act.wait_ge(x_turned, j + 1)
                act.activation(k.x_t[:, 4 * half:4 * half + 4, t * P:t * P + rows],
                               ps[j % 4][:, :].rearrange("p (c n) -> p c n", c=4)[:, :, 0:rows],
                               ACT.Copy).then_inc(x_free, 1)

        @block.vector
        def _(dve):
            own = Tally(dve, dve_own)
            own.do(dve.memset(c_t[:, :, :], 0.0))
            dve.wait_ge(act_own, 1)
            own.do(dve.tensor_scalar(c_e[:, :], c_e[:, :], 1.0, None, ALU.add))
            own.do(dve.reciprocal(c_e[:, :], c_e[:, :]))
            dve.tensor_tensor(c_rows[:, :], c_rows[:, :], c_e[:, :], ALU.mult).then_inc(c_done, 1)
            dve.wait_ge(c_turned, 1)
            dve.tensor_copy(c_t[:, :, 0:9], ps[4][:, 0:NC * 16].rearrange("p (c n) -> p c n", c=NC)[:, :, 0:9]
                            ).then_inc(c_done, 1)
            dve.wait_ge(v_turned, 1)
            own.do(dve.tensor_copy(k.vec_t[:, 0:96], ps[7][:, 256:352]))
            own.do(dve.tensor_copy(k.vec_t[:, 96:168], ps[7][:, 384:456]))
            for j in range(0, XJOBS, 2):
                t, half = j // 2, j % 2
                rows = P if t < 8 else TS
                dve.wait_ge(x_turned, j + 1)
                dve.tensor_copy(k.x_t[:, 4 * half:4 * half + 4, t * P:t * P + rows],
                                ps[j % 4][:, :].rearrange("p (c n) -> p c n", c=4)[:, :, 0:rows]).then_inc(x_kept, 1)
            for n in range(2 * NIT):
                layer, it = divmod(n, NIT)
                dve.wait_ge(ada_used, 4 + NC * (n + 1))
                dve.tensor_copy(mod_rows[:, n % 2, :], ps[5][:, :]).then_inc(mod_kept, 1)
                dve.wait_ge(mod_turned, n + 1)
                out = k.mod[layer][:, 16 * it:16 * it + 16, :].rearrange("p (g j) r -> p j g r", g=4)
                dve.tensor_tensor(
                    out, ps[6][:, :].rearrange("p (j g r) -> p j g r", j=4, g=4)[:, :, :, 0:9],
                    over(k.b_ada[layer][:, 16 * it:16 * it + 16].rearrange("p (g j) -> p j g", g=4), 9),
                    ALU.add).then_inc(mod_out, 1)
            dve.wait_ge(mod_out, 2 * NIT)
            for layer in range(2):
                m = k.mod[layer]
                for scale in (1, 4):
                    own.mark(dve.tensor_scalar(m[:, 8 * scale:8 * scale + 8, :], m[:, 8 * scale:8 * scale + 8, :],
                                               1.0, None, ALU.add))
                for gate in (2, 5):
                    own.mark(dve.tensor_scalar(m[:, 8 * gate:8 * gate + 8, :], m[:, 8 * gate:8 * gate + 8, :],
                                               1.0 / ALPHA, None, ALU.mult))
            own.settle()
            own.do(dve.tensor_tensor(k.mod[0][:, 16:24, :], k.mod[0][:, 16:24, :], over(k.pool_scale, 9), ALU.mult))
            dve.wait_ge(made, MADE)
            dve.wait_ge(b_in, 32)
            own.do(dve.tensor_reduce(k.block_of[:, :], k.head_of[:, :].rearrange("p (g h) -> p h g", g=4), AX.X, ALU.add))
            own.do(dve.tensor_tensor(k.head_of[:, :], k.head_of[:, :], k.bias_all[:, :], ALU.mult))
            own.do(dve.tensor_reduce(k.bias_row[:, :], k.head_of[:, :], AX.X, ALU.add))

        @block.tensor
        def _(pe):
            pe.sem_inc(ada_used, 4)
            pe.wait_ge(made, 2)
            pe.wait_ge(c_done, 1)
            for c in range(NC):
                last = pe.transpose(ps[4][:, 16 * c:16 * c + 9], c_rows[0:9, c * P:(c + 1) * P], k.ident[0:9, 0:9])
            last.then_inc(c_turned, 1)
            pe.wait_ge(v_in, 64)
            pe.transpose(ps[7][:, 256:352], vec_rows[0:96, 0, :], k.ident[0:96, 0:96])
            pe.transpose(ps[7][:, 384:456], vec_rows[0:72, 1, :], k.ident[0:72, 0:72]).then_inc(v_turned, 1)
            pe.wait_ge(x_in, 32)
            for j in range(XJOBS):
                t, half = j // 2, j % 2
                rows = P if t < 8 else TS
                if j >= 4:
                    pe.wait_ge(x_free if j % 2 else x_kept, (j - 4) // 2 + 1)
                for c in range(4):
                    last = pe.transpose(ps[j % 4][:, c * P:c * P + rows],
                                        x_rows[0:rows, t, (4 * half + c) * P:(4 * half + c + 1) * P],
                                        k.ident[0:rows, 0:rows])
                last.then_inc(x_turned, 1)
            pe.wait_ge(c_done, 2)
            for n in range(2 * NIT):
                if n:
                    pe.wait_ge(mod_kept, n)
                for c in range(NC):
                    pe.wait_ge(w_in[c % 4], 16 * (2 * n + c // 4 + 1))
                    for g in range(4):
                        last = pe.matmul(ps[5][32 * g:32 * g + 32, :], c_t[:, c, :],
                                         w_raw[:, c % 4, 512 * g:512 * g + 512], start=(c == 0), stop=(c == NC - 1),
                                         tile_position=(0, 32 * g), skip_group_check=True)
                    last.then_inc(ada_used, 1)
                pe.wait_ge(mod_kept, n + 1)
                if n:
                    pe.wait_ge(mod_out, n)
                for j in range(4):
                    last = pe.transpose(ps[6][:, j * P:(j + 1) * P], mod_rows[:, n % 2, j * P:(j + 1) * P],
                                        k.ident[:, :])
                last.then_inc(mod_turned, 1)


def gated_add(dve, own, k, layer, gate, m, piece, psum, tmp, free):
    c0, w = PIECES[piece]
    wp = w if piece < 2 else LASTP
    g = k.mod[layer]
    if piece == 2:
        x = k.x_t[:, m, TP:T]
        t = tmp[:, 0:TS]
        own.settle()
        own.do(dve.tensor_tensor(t.rearrange("p (b t) -> p b t", b=DB),
                                 psum[:, wp:w].rearrange("p (b t) -> p b t", b=DB),
                                 over(g[:, 8 * gate + m, 1:9], DS), ALU.mult))
        own.mark(dve.tensor_tensor(x, x, t, ALU.add))
    x = k.x_t[:, m, c0:c0 + wp]
    dve.scalar_tensor_tensor(out=x, in0=psum[:, 0:wp], scalar=g[:, 8 * gate + m, 0:1], in1=x,
                             op0=ALU.mult, op1=ALU.add).then_inc(free, 1)


def modulate_sample(dve, own, k, layer, scale, shift, x, out):
    m = k.mod[layer]
    x4 = x.rearrange("p c (b t) -> p c b t", b=DB)
    o4 = out.rearrange("p c (b t) -> p c b t", b=DB)
    own.do(dve.tensor_tensor(o4, x4, over(m[:, 8 * scale:8 * scale + 8, 1:9], DS), ALU.mult))
    own.do(dve.tensor_tensor(o4, o4, over(m[:, 8 * shift:8 * shift + 8, 1:9], DS), ALU.add))


def norm(nc, k, name, layer, which, to):
    with ExitStack() as ctx:
        squares = k.at("norm_sq", [P, 3, NC, 364], F32, k.WORK_AT)
        h_full = k.at("norm_h", [P, NC, 364], F32, k.WORK_AT + 3 * NC * 364 * 4)
        inv_var = k.at("norm_inv", [P, 364], F32, k.WORK_AT + 4 * NC * 364 * 4)
        rstd = k.at("norm_rstd", [P, 364], F32, k.WORK_AT + 4 * NC * 364 * 4 + 1472)
        mu_done, centred, squared, var_done, dve_own, normed, h_done, h_split, inv_done, rstd_done = sems(
            ctx, nc, name, "mu_done", "centred", "squared", "var_done", "dve_own", "normed", "h_done", "h_split",
            "inv_done", "rstd_done")
        block = ctx.enter_context(nc.Block())
        gain, bias = k.ln_g[layer][which], k.ln_b[layer][which]

        @block.tensor
        def _(pe):
            for s, (c0, w) in enumerate(PIECES):
                for m in range(NC):
                    last = pe.matmul(k.ps[s][:, 0:w], k.mean_of[:, :], k.x_t[:, m, c0:c0 + w],
                                     start=(m == 0), stop=(m == NC - 1))
                last.then_inc(mu_done, 1)
            for s, (c0, w) in enumerate(PIECES):
                pe.wait_ge(squared, s + 1)
                for m in range(NC):
                    last = pe.matmul(k.ps[3 + s][:, 0:w], k.mean_of[:, :], squares[:, s, m, 0:w],
                                     start=(m == 0), stop=(m == NC - 1))
                last.then_inc(var_done, 1)

        @block.vector
        def _(dve):
            own = Tally(dve, dve_own)
            for s, (c0, w) in enumerate(PIECES):
                dve.wait_ge(mu_done, s + 1)
                x = k.x_t[:, :, c0:c0 + w]
                dve.tensor_tensor(x, x, k.ps[s][:, 0:w].unsqueeze(1).to_broadcast([P, NC, w]),
                                  ALU.subtract).then_inc(centred, 1)
            dve.wait_ge(centred, 3)
            for s, (c0, w) in enumerate(PIECES):
                x = k.x_t[:, :, c0:c0 + w]
                dve.wait_ge(var_done, s + 1)
                if s:
                    own.settle()
                own.do(dve.tensor_scalar(inv_var[:, 0:w], k.ps[3 + s][:, 0:w], EPS, None, ALU.add))
                dve.reciprocal(inv_var[:, 0:w], inv_var[:, 0:w]).then_inc(inv_done, 1)
                dve.wait_ge(rstd_done, s + 1)
                dve.wait_ge(squared, s + 1)
                own.do(dve.tensor_tensor(x, x, rstd[:, 0:w].unsqueeze(1).to_broadcast([P, NC, w]), ALU.mult))
                for m in range(NC):
                    last = dve.tensor_scalar(k.x_t[:, m, c0:c0 + w], k.x_t[:, m, c0:c0 + w], gain[:, m:m + 1],
                                             bias[:, m:m + 1], ALU.mult, ALU.add)
                last.then_inc(normed, 1)
                if to is None:
                    continue
                dve.wait_ge(normed, s + 1)
                hi, lo = k.hi[:, :, c0:c0 + w], k.lo[:, :, c0:c0 + w]
                full = x
                if to != "x":
                    full = h_full[:, :, 0:w]
                    if s == 2:
                        modulate_sample(dve, own, k, *to, k.x_t[:, :, TP:T], h_full[:, :, LASTP:w])
                    dve.wait_ge(h_done, s + 1)
                own.do(dve.tensor_copy(hi, full))
                dve.tensor_tensor(lo, full, hi.bitcast(F32), ALU.subtract).then_inc(h_split, 1)

        @block.scalar
        def _(act):
            for s, (c0, w) in enumerate(PIECES):
                act.wait_ge(centred, s + 1)
                act.activation(squares[:, s, :, 0:w], k.x_t[:, :, c0:c0 + w], ACT.Square).then_inc(squared, 1)
            for s, (c0, w) in enumerate(PIECES):
                wp = w if s < 2 else LASTP
                act.wait_ge(inv_done, s + 1)
                if s:
                    act.wait_ge(normed, s)
                act.activation(rstd[:, 0:w], inv_var[:, 0:w], ACT.Sqrt).then_inc(rstd_done, 1)
                if to in (None, "x"):
                    continue
                layer_, scale, shift = to
                act.wait_ge(normed, s + 1)
                if s:
                    act.wait_ge(h_split, s)
                for m in range(NC):
                    last = act.activation(h_full[:, m, 0:wp], k.x_t[:, m, c0:c0 + wp], ACT.Identity,
                                          bias=k.mod[layer_][:, 8 * shift + m, 0:1],
                                          scale=k.mod[layer_][:, 8 * scale + m, 0:1])
                last.then_inc(h_done, 1)


def modulate(nc, k, name, layer, scale, shift):
    with ExitStack() as ctx:
        h_full = k.at("mod_h", [P, 2, NC, 364], F32, k.WORK_AT)
        h_done, h_split, dve_own = sems(ctx, nc, name, "h_done", "h_split", "dve_own")
        block = ctx.enter_context(nc.Block())

        @block.scalar
        def _(act):
            for s, (c0, w) in enumerate(PIECES):
                wp = w if s < 2 else LASTP
                if s >= 2:
                    act.wait_ge(h_split, s - 1)
                for m in range(NC):
                    last = act.activation(h_full[:, s % 2, m, 0:wp], k.x_t[:, m, c0:c0 + wp], ACT.Identity,
                                          bias=k.mod[layer][:, 8 * shift + m, 0:1],
                                          scale=k.mod[layer][:, 8 * scale + m, 0:1])
                last.then_inc(h_done, 1)

        @block.vector
        def _(dve):
            own = Tally(dve, dve_own)
            for s, (c0, w) in enumerate(PIECES):
                full = h_full[:, s % 2, :, 0:w]
                hi, lo = k.hi[:, :, c0:c0 + w], k.lo[:, :, c0:c0 + w]
                if s == 2:
                    dve.wait_ge(h_split, 1)
                    modulate_sample(dve, own, k, layer, scale, shift, k.x_t[:, :, TP:T], full[:, :, LASTP:w])
                dve.wait_ge(h_done, s + 1)
                own.do(dve.tensor_copy(hi, full))
                dve.tensor_tensor(lo, full, hi.bitcast(F32), ALU.subtract).then_inc(h_split, 1)


def pool_mixer(nc, k, a):
    with ExitStack() as ctx:
        o = k.WORK_AT
        HW = 16 + TP
        h_p = k.at("pm_hp", [P, 2, HW], F32, o)
        s_p = k.at("pm_sp", [P, 2, HW], F32, o + 2 * HW * 4)
        o += 4 * HW * 4
        h_s = k.at("pm_hs", [P, 2, DB, 24], F32, o)
        s_s = k.at("pm_ss", [P, 2, DB, 24], F32, o + 1536)
        d = k.at("pm_d", [P, T], F32, o + 3072)
        o += 3072 + T * 4
        w_raw = k.at("pm_wraw", [P, 4, 2, 256], F32, o)
        w_hi = k.at("pm_whi", [P, 4, 2, 256], F32R, o + 8192)
        w_lo = k.at("pm_wlo", [P, 4, 2, 256], F32R, o + 16384)
        o += 24576
        tail_p = k.at("pm_tp", [P, NC, HIST], F32, o)
        tail_s = k.at("pm_ts", [P, NC, TS], F32, o + 480)
        tmp = k.at("pm_tmp", [P, TS], F32, o + 480 + 2048)
        o += 480 + 2048 + 256
        hist = k.at("pm_hist", [P, D], F32, k.F_AT)
        out_p = k.at("pm_op", [P, D], F32, k.F_AT + 4096)
        out_s = k.at("pm_os", [P, D], F32, k.F_AT + 8192)
        (hist_in, w_in, hist_turned, h_done, h_used, dve_own, d_done, hi_done, whi_done, w_done, mixed, free,
         tails, turned, kept, stored, zeroed) = sems(
            ctx, nc, "pm", "hist_in", "w_in", "hist_turned", "h_done", "h_used", "dve_own", "d_done", "hi_done",
            "whi_done", "w_done", "mixed", "free", "tails", "turned", "kept", "stored", "zeroed")
        block = ctx.enter_context(nc.Block())
        ps = k.ps

        @block.sync
        def _(sp):
            sp.dma_start(hist[0:DB * HIST, :], a["state_pool"][0].rearrange("b r d -> (b r) d")).then_inc(hist_in, 16)
            sp.dma_start(w_raw[:, :, :, :], a["w_pool"][0].rearrange("g (c p) n -> p g c n", p=P)).then_inc(w_in, 16)
            sp.dma_start(a["pool_sample"][0, :, 0:HIST - DS, :], a["state_pool"][0, :, DS:HIST, :]).then_inc(stored, 16)
            sp.wait_ge(kept, 2)
            sp.dma_start(a["pool_prompt"][0, 0], out_p[0:HIST, :]).then_inc(stored, 16)
            sp.wait_ge(kept, 4)
            sp.dma_start(a["pool_sample"][0, :, HIST - DS:HIST, :], out_s[0:TS, :]).then_inc(stored, 16)
            sp.wait_ge(stored, 48)

        @block.scalar
        def _(act):
            act.wait_ge(w_in, 16)
            act.activation(w_hi[:, :, :, :], w_raw[:, :, :, :], ACT.Copy).then_inc(whi_done, 1)
            for c in range(NC):
                if c >= 2:
                    act.wait_ge(h_used, c - 1)
                act.activation(h_p[:, c % 2, 16:HW], k.x_t[:, c, 0:TP], ACT.Identity,
                               bias=k.mod[0][:, c, 0:1], scale=k.mod[0][:, 8 + c, 0:1]).then_inc(h_done, 1)

        @block.vector
        def _(dve):
            own = Tally(dve, dve_own)
            own.mark(dve.memset(h_p[:, :, 0:16], 0.0))
            own.do(dve.memset(h_s[:, :, :, 0:1], 0.0))
            dve.wait_ge(whi_done, 1)
            dve.tensor_tensor(w_lo[:, :, :, :], w_raw[:, :, :, :], w_hi[:, :, :, :].bitcast(F32),
                              ALU.subtract).then_inc(w_done, 1)
            dve.wait_ge(hist_turned, 1)

            def chunk(c):
                win = WIN[c // 2]
                b = c % 2
                hs, hp = h_s[:, b, :, :], h_p[:, b, :]
                x = k.x_t[:, c, TP:T].rearrange("p (b t) -> p b t", b=DB)
                own.mark(dve.tensor_copy(hs[:, :, 1:16],
                                         ps[6 + c // 4][:, (c % 4) * P:(c % 4) * P + DB * HIST]
                                         .rearrange("p (b r) -> p b r", b=DB)))
                own.do(dve.tensor_tensor(hs[:, :, 16:24], x, over(k.mod[0][:, 8 + c, 1:9], DS), ALU.mult))
                own.do(dve.tensor_tensor(hs[:, :, 16:24], hs[:, :, 16:24], over(k.mod[0][:, c, 1:9], DS), ALU.add))
                own.mark(dve.tensor_copy(tail_s[:, c, :].rearrange("p (b t) -> p b t", b=DB), hs[:, :, 16:24]))
                dve.wait_ge(h_done, c + 1)
                own.mark(dve.tensor_copy(tail_p[:, c, :], hp[:, HW - HIST:HW]))
                src_p, src_s, step, lo, n = hp, hs, 1, 1, 0
                while step < win:
                    dst_p, dst_s = s_p[:, n % 2, :], s_s[:, n % 2, :, :]
                    own.mark(dve.tensor_tensor(dst_p[:, lo:HW], src_p[:, lo:HW], src_p[:, lo - step:HW - step], ALU.add))
                    own.do(dve.tensor_tensor(dst_s[:, :, lo:24], src_s[:, :, lo:24], src_s[:, :, lo - step:24 - step],
                                             ALU.add))
                    src_p, src_s, step, n = dst_p, dst_s, 2 * step, n + 1
                    lo += step
                if c:
                    dve.wait_ge(hi_done, c)
                own.mark(dve.scalar_tensor_tensor(out=d[:, win - 1:TP], in0=src_p[:, 15 + win:HW], scalar=1.0 / win,
                                                  in1=hp[:, 15 + win:HW], op0=ALU.mult, op1=ALU.subtract))
                own.mark(dve.scalar_tensor_tensor(out=d[:, TP:T].rearrange("p (b t) -> p b t", b=DB),
                                                  in0=src_s[:, :, 16:24], scalar=1.0 / win, in1=hs[:, :, 16:24],
                                                  op0=ALU.mult, op1=ALU.subtract))
                own.do(dve.tensor_tensor(d[:, 0:win - 1], src_p[:, 16:15 + win], k.inv_seen[:, 0:win - 1], ALU.mult))
                own.do(dve.tensor_tensor(d[:, 0:win - 1], d[:, 0:win - 1], hp[:, 16:15 + win], ALU.subtract))
                dve.tensor_copy(k.hi[:, c, :], d[:, :]).then_inc(h_used, 1)
                dve.wait_ge(h_used, c + 1)
                dve.tensor_tensor(k.lo[:, c, :], d[:, :], k.hi[:, c, :].bitcast(F32), ALU.subtract).then_inc(hi_done, 1)

            for c in range(NC):
                chunk(c)
                if c % 2:
                    for j in range(6 * (c // 2), 6 * (c // 2) + 6):
                        m, s = divmod(j, 3)
                        dve.wait_ge(mixed, j + 1)
                        gated_add(dve, own, k, 0, 2, m, s, ps[j % 4], tmp, free)
            own.settle()
            dve.tensor_copy(tmp[:, 0:1], tail_s[:, 0, 0:1]).then_inc(tails, 1)
            for half in range(2):
                dve.wait_ge(turned, half + 1)
                dve.tensor_copy(out_p[0:HIST, 512 * half:512 * half + 512], ps[4 + half][0:HIST, :]).then_inc(kept, 1)
            for half in range(2):
                dve.wait_ge(turned, half + 3)
                dve.tensor_copy(out_s[0:TS, 512 * half:512 * half + 512], ps[6 + half][0:TS, :]).then_inc(kept, 1)

        @block.tensor
        def _(pe):
            pe.wait_ge(hist_in, 16)
            for c in range(NC):
                last = pe.transpose(ps[6 + c // 4][:, (c % 4) * P:(c % 4) * P + DB * HIST],
                                    hist[0:DB * HIST, c * P:(c + 1) * P], k.ident[0:DB * HIST, 0:DB * HIST])
            last.then_inc(hist_turned, 1)
            pe.wait_ge(w_done, 1)
            for j in range(24):
                m, s = divmod(j, 3)
                g = m // 2
                c0, w = PIECES[s]
                pe.wait_ge(hi_done, 2 * g + 2)
                if j >= 4:
                    pe.wait_ge(free, j - 3)
                for c in range(2):
                    col = (m % 2) * P
                    last = three(pe, ps[j % 4][:, 0:w], w_hi[:, g, c, col:col + P], w_lo[:, g, c, col:col + P],
                                 k.hi[:, 2 * g + c, c0:c0 + w], k.lo[:, 2 * g + c, c0:c0 + w], c == 0, c == 1)
                last.then_inc(mixed, 1)
            pe.wait_ge(tails, 1)
            for rows, tail, bank in ((HIST, tail_p, 4), (TS, tail_s, 6)):
                for c in range(NC):
                    last = pe.transpose(ps[bank + c // 4][0:rows, (c % 4) * P:(c % 4 + 1) * P], tail[:, c, :],
                                        k.ident[:, :])
                    if c % 4 == 3:
                        last.then_inc(turned, 1)


def mlp(nc, k, name, layer, w_up, w_down):
    NB, FC, JOBS, BANKS, TILES = DFF // 512, 4, 36, 6, 8
    with ExitStack() as ctx:
        o = k.WORK_AT
        raw = k.at("mlp_raw", [P, 2, D], F32, o)
        up_hi = k.at("mlp_uphi", [P, 2, NC, P], F32R, o + 8192)
        up_lo = k.at("mlp_uplo", [P, 2, NC, P], F32R, o + 16384)
        dn_hi = k.at("mlp_dnhi", [P, FC, D], F32R, o + 24576)
        dn_lo = k.at("mlp_dnlo", [P, FC, D], F32R, o + 40960)
        f = k.at("mlp_f", [P, 2, 364], F32, o + 57344)
        tmp = k.at("mlp_tmp", [P, TS], F32, o + 57344 + 2912)
        f_hi = k.at("mlp_fhi", [P, FC, T], F32R, k.F_AT)
        f_lo = k.at("mlp_flo", [P, FC, T], F32R, k.F_AT + FC * T * 4)
        w_hi_done, w_done, job_done, bank_free, dve_own = sems(
            ctx, nc, name, "w_hi_done", "w_done", "job_done", "bank_free", "dve_own")
        raw_in = sems(ctx, nc, name, "raw_in0", "raw_in1")
        block = ctx.enter_context(nc.Block())
        up = w_up[layer].rearrange("(k p) n -> p k n", p=P)
        down = w_down[layer]
        ORDER = [("down", 0), ("up", 2), ("down", 1), ("up", 3), ("down", 2), ("down", 3), ("next", 0), ("next", 1)]

        def split_target(kind, c):
            if kind == "down":
                return dn_hi[:, c, :], dn_lo[:, c, :]
            return (up_hi[:, c % 2, :, :].rearrange("p k n -> p (k n)"),
                    up_lo[:, c % 2, :, :].rearrange("p k n -> p (k n)"))

        @block.sync
        def _(sp):
            def load(n, slot, kind, c, i):
                sp.wait_ge(w_done, n + 1)
                if kind == "down":
                    src, dst = down[bass.ds((i * FC + c) * P, P), :], raw[:, slot, :]
                else:
                    src = up[:, :, bass.ds((i * FC + c) * P, P)]
                    dst = raw[:, slot, :].rearrange("p (k n) -> p k n", k=NC)
                sp.dma_start(dst, src).then_inc(raw_in[slot], 16)
            load(0, 0, "up", 0, 0)
            load(1, 1, "up", 1, 0)
            with sp.Fori(0, NB - 1) as i:
                for r, (kind, c) in enumerate(ORDER):
                    load(i * TILES + (2 + r), r % 2, kind, c, i + 1 if kind == "next" else i)
            for r, (kind, c) in enumerate(ORDER[:6]):
                load((NB - 1) * TILES + 2 + r, r % 2, kind, c, NB - 1)

        @block.scalar
        def _(act):
            def hi_half(i, r, kind, c):
                before = {"down": 0, "up": 3 * (c - 1), "next": 9 + 3 * (c % 2)}[kind]
                act.wait_ge(raw_in[r % 2], i * (TILES // 2 * 16) + 16 * ((2 + r) // 2 + 1))
                act.wait_ge(job_done, i * JOBS + (before + 1))
                act.activation(split_target(kind, c)[0], raw[:, r % 2, :], ACT.Copy).then_inc(w_hi_done, 1)
            for c in range(2):
                act.wait_ge(raw_in[c], 16)
                act.activation(split_target("up", c)[0], raw[:, c, :], ACT.Copy).then_inc(w_hi_done, 1)
            with act.Fori(0, NB - 1) as i:
                for r, (kind, c) in enumerate(ORDER):
                    hi_half(i, r, kind, c)
            for r, (kind, c) in enumerate(ORDER[:6]):
                hi_half(NB - 1, r, kind, c)

        @block.gpsimd
        def _(pool):
            def lo_half(n, slot, kind, c):
                hi, lo = split_target(kind, c)
                pool.wait_ge(w_hi_done, n + 1)
                pool.tensor_tensor(lo, raw[:, slot, :], hi.bitcast(F32), ALU.subtract).then_inc(w_done, 1)
            pool.sem_inc(w_done, 2)
            lo_half(0, 0, "up", 0)
            lo_half(1, 1, "up", 1)
            with pool.Fori(0, NB - 1) as i:
                for r, (kind, c) in enumerate(ORDER):
                    lo_half(i * TILES + (2 + r), r % 2, kind, c)
            for r, (kind, c) in enumerate(ORDER[:6]):
                lo_half((NB - 1) * TILES + 2 + r, r % 2, kind, c)

        @block.vector
        def _(dve):
            own = Tally(dve, dve_own)
            with dve.Fori(0, NB) as i:
                own.base, own.k = i * (36 + 16), 0
                for j in range(12):
                    c, s = divmod(j, 3)
                    c0, w = PIECES[s]
                    dve.wait_ge(job_done, i * JOBS + (j + 2))
                    u = k.ps[j % BANKS][:, 0:w]
                    ft = f[:, j % 2, 0:w]
                    own.do(dve.tensor_scalar(ft, u, 0.0, None, ALU.max))
                    own.do(dve.tensor_tensor(ft, ft, ft, ALU.mult))
                    hi = f_hi[:, c, c0:c0 + w]
                    own.do(dve.tensor_copy(hi, ft))
                    dve.tensor_tensor(f_lo[:, c, c0:c0 + w], ft, hi.bitcast(F32), ALU.subtract).then_inc(bank_free, 1)
                dve.wait_ge(bank_free, i * JOBS + (BANKS + 12))
                for j in range(12, JOBS):
                    s, m = divmod(j - 12, NC)
                    dve.wait_ge(job_done, i * JOBS + (j + 2))
                    gated_add(dve, own, k, layer, 5, m, s, k.ps[j % BANKS], tmp, bank_free)

        @block.tensor
        def _(pe):
            pe.sem_inc(bank_free, BANKS)
            pe.sem_inc(job_done, 1)
            with pe.Fori(0, NB) as i:
                for j in range(JOBS):
                    pe.wait_ge(bank_free, i * JOBS + (j + 1))
                    if j < 12:
                        c, s = divmod(j, 3)
                        c0, w = PIECES[s]
                        if s == 0:
                            pe.wait_ge(w_done, i * TILES + (2 + (1, 2, 4, 6)[c]))
                        for q in range(NC):
                            last = three(pe, k.ps[j % BANKS][:, 0:w], up_hi[:, c % 2, q, :], up_lo[:, c % 2, q, :],
                                         k.hi[:, q, c0:c0 + w], k.lo[:, q, c0:c0 + w], q == 0, q == NC - 1)
                    else:
                        s, m = divmod(j - 12, NC)
                        c0, w = PIECES[s]
                        if m == 0:
                            if s == 0:
                                pe.wait_ge(w_done, i * TILES + (2 + 8))
                            pe.wait_ge(bank_free, i * JOBS + (BANKS + 10 + s))
                        for q in range(FC):
                            last = three(pe, k.ps[j % BANKS][:, 0:w], dn_hi[:, q, m * P:(m + 1) * P],
                                         dn_lo[:, q, m * P:(m + 1) * P], f_hi[:, q, c0:c0 + w],
                                         f_lo[:, q, c0:c0 + w], q == 0, q == FC - 1)
                    last.then_inc(job_done, 1)


def keys_values(nc, k, a):
    NBLK, W, TILES, BANKS = 8, 256, 9, 6
    with ExitStack() as ctx:
        o = k.WORK_AT
        raw = k.at("kv_raw", [P, 2, NC, W], F32, o)
        w_hi = k.at("kv_hi", [P, 2, NC, W], F32R, o + 16384)
        w_lo = k.at("kv_lo", [P, 2, NC, W], F32R, o + 32768)
        stage = k.at("kv_stage", [P, BANKS, W], F32, o + 49152)
        w_hi_done, w_done, job_done, kept = sems(ctx, nc, "kv", "w_hi_done", "w_done", "job_done", "kept")
        raw_in = sems(ctx, nc, "kv", "raw_in0", "raw_in1")
        stored = sems(ctx, nc, "kv", *[f"stored{j}" for j in range(BANKS)])
        block = ctx.enter_context(nc.Block())
        w = a["w_kv"].rearrange("(k p) n -> p k n", p=P)

        @block.sync
        def _(sp):
            for j in range(BANKS):
                sp.sem_inc(stored[j], 16)
            for n in range(2):
                sp.dma_start(raw[:, n, :, :], w[:, :, n * W:(n + 1) * W]).then_inc(raw_in[n], 16)

            def blocks(kv, i, ahead):
                kp = (a["k_prompt"], a["v_prompt"])[kv][0].rearrange("t h d -> t (h d)")
                ks = (a["k_sample"], a["v_sample"])[kv].rearrange("b t h d -> (b t) (h d)")
                for n in range(2):
                    for t in range(TILES):
                        j = n * TILES + t
                        rows = P if t < 8 else TS
                        dst = kp[t * P:(t + 1) * P, :] if t < 8 else ks
                        sp.wait_ge(kept, i * 18 + (36 * kv + BANKS + j + 1))
                        sp.dma_start(dst[:, bass.ds((i * 2 + n) * W, W)], stage[0:rows, j % BANKS, :]
                                     ).then_inc(stored[j % BANKS], 16)
                    if ahead:
                        sp.wait_ge(w_done, i * 2 + (4 * kv + n + 3))
                        sp.dma_start(raw[:, n, :, :], w[:, :, bass.ds((i * 2 + (4 * kv + n + 2)) * W, W)]
                                     ).then_inc(raw_in[n], 16)
            with sp.Fori(0, 2) as i:
                blocks(0, i, True)
            blocks(1, 0, True)
            blocks(1, 1, False)
            for j in range(BANKS):
                sp.wait_ge(stored[j], 16 * (72 // BANKS + 1))

        @block.scalar
        def _(act):
            with act.Fori(0, 4) as i:
                for n in range(2):
                    act.wait_ge(raw_in[n], i * 16 + 16)
                    act.wait_ge(job_done, i * 18 + (n * 9 + 9))
                    act.activation(w_hi[:, n, :, :], raw[:, n, :, :], ACT.Copy).then_inc(w_hi_done, 1)

        @block.gpsimd
        def _(pool):
            pool.sem_inc(w_done, 2)
            with pool.Fori(0, 4) as i:
                for n in range(2):
                    pool.wait_ge(w_hi_done, i * 2 + (n + 1))
                    pool.tensor_tensor(w_lo[:, n, :, :], raw[:, n, :, :], w_hi[:, n, :, :].bitcast(F32),
                                       ALU.subtract).then_inc(w_done, 1)

        @block.vector
        def _(dve):
            with dve.Fori(0, 4) as i:
                for j in range(18):
                    rows = P if j % TILES < 8 else TS
                    dve.wait_ge(job_done, i * 18 + (18 + j + 1))
                    dve.wait_ge(stored[j % BANKS], i * 48 + 16 * (j // BANKS + 1))
                    dve.tensor_copy(stage[0:rows, j % BANKS, :], k.ps[j % BANKS][0:rows, 0:W]).then_inc(kept, 1)

        @block.tensor
        def _(pe):
            pe.sem_inc(job_done, 18)
            pe.sem_inc(kept, BANKS)
            with pe.Fori(0, 4) as i:
                for j in range(18):
                    n, t = divmod(j, TILES)
                    rows = P if t < 8 else TS
                    if t == 0:
                        pe.wait_ge(w_done, i * 2 + (2 + n + 1))
                    pe.wait_ge(kept, i * 18 + (j + 1))
                    for q in range(NC):
                        x_hi, x_lo = k.hi[:, q, t * P:t * P + rows], k.lo[:, q, t * P:t * P + rows]
                        last = three(pe, k.ps[j % BANKS][0:rows, 0:W], x_hi, x_lo, w_hi[:, n, q, :],
                                     w_lo[:, n, q, :], q == 0, q == NC - 1)
                    last.then_inc(job_done, 1)


def project(nc, k, name, w_dram, to_query):
    BANKS = 6
    with ExitStack() as ctx:
        o = k.WORK_AT
        raw = k.at("proj_raw", [P, 2, NC, P], F32, o)
        w_hi = k.at("proj_hi", [P, 2, NC, P], F32R, o + 8192)
        w_lo = k.at("proj_lo", [P, 2, NC, P], F32R, o + 16384)
        tmp = k.at("proj_tmp", [P, TS], F32, o + 24576)
        w_hi_done, w_done, job_done, bank_free, dve_own = sems(
            ctx, nc, name, "w_hi_done", "w_done", "job_done", "bank_free", "dve_own")
        raw_in = sems(ctx, nc, name, "raw_in0", "raw_in1")
        block = ctx.enter_context(nc.Block())
        w = w_dram[0].rearrange("(k p) n -> p k n", p=P)

        @block.sync
        def _(sp):
            with sp.Fori(0, 4) as i:
                for n in range(2):
                    sp.wait_ge(w_done, i * 2 + (n + 1))
                    sp.dma_start(raw[:, n, :, :], w[:, :, bass.ds((i * 2 + n) * P, P)]).then_inc(raw_in[n], 16)

        @block.scalar
        def _(act):
            with act.Fori(0, 4) as i:
                for n in range(2):
                    act.wait_ge(raw_in[n], i * 16 + 16)
                    act.wait_ge(job_done, i * 6 + (n * 3 + 3))
                    act.activation(w_hi[:, n, :, :], raw[:, n, :, :], ACT.Copy).then_inc(w_hi_done, 1)

        @block.gpsimd
        def _(pool):
            pool.sem_inc(w_done, 2)
            with pool.Fori(0, 4) as i:
                for n in range(2):
                    pool.wait_ge(w_hi_done, i * 2 + (n + 1))
                    pool.tensor_tensor(w_lo[:, n, :, :], raw[:, n, :, :], w_hi[:, n, :, :].bitcast(F32),
                                       ALU.subtract).then_inc(w_done, 1)

        @block.vector
        def _(dve):
            own = Tally(dve, dve_own)
            for j in range(24):
                m, s = divmod(j, 3)
                c0, w_ = PIECES[s]
                dve.wait_ge(job_done, 6 + j + 1)
                if to_query:
                    dve.tensor_scalar(k.q_t[:, m, c0:c0 + w_], k.ps[j % BANKS][:, 0:w_], HD ** -0.5, None,
                                      ALU.mult).then_inc(bank_free, 1)
                else:
                    gated_add(dve, own, k, 1, 2, m, s, k.ps[j % BANKS], tmp, bank_free)

        @block.tensor
        def _(pe):
            pe.sem_inc(job_done, 6)
            pe.sem_inc(bank_free, BANKS)
            with pe.Fori(0, 4) as i:
                for j in range(6):
                    n, s = divmod(j, 3)
                    c0, w_ = PIECES[s]
                    if s == 0:
                        pe.wait_ge(w_done, i * 2 + (2 + n + 1))
                    pe.wait_ge(bank_free, i * 6 + (j + 1))
                    for q in range(NC):
                        last = three(pe, k.ps[j % BANKS][:, 0:w_], w_hi[:, n, q, :], w_lo[:, n, q, :],
                                     k.hi[:, q, c0:c0 + w_], k.lo[:, q, c0:c0 + w_], q == 0, q == NC - 1)
                    last.then_inc(job_done, 1)


def attend_sample(nc, k, a):
    with ExitStack() as ctx:
        o = k.HH_AT
        k_t = k.at("sa_kt", [P, NC, 512], F32, o)
        k_page = k.at("sa_kpage", [P, 4, D], F32, o + 16384)
        z_rows = k.at("sa_zrows", [P, 512], F32, o + 32768)
        t = k.at("sa_t", [P, 512], F32, o + 34816)
        spl = k.at("sa_sp", [P, 2, 4, P], F32, o + 36864)
        att = k.at("sa_a", [P, 2, 512], F32, o + 40960)
        behind = k.at("sa_behind", [P, 2, 4, P], F32, o + 45056)
        q_tiles = k.at("sa_q", [P, NC, 32], F32, o + 49152)
        o_part = k.at("sa_op", [P, 4, HD], F32, o + 50176)
        o_rows = k.at("sa_or", [P, P], F32, o + 51200)
        v_page = k.at("sa_vpage", [P, 8, D], F32, k.WORK_AT)
        k_new = k.at("sa_knew", [P, D], F32, k.WORK_AT + 32768)
        v_new = k.at("sa_vnew", [P, D], F32, k.WORK_AT + 36864)
        (zeroed, kn_in, vn_in, k_turned, act_kept, dve_kept, z_done, z_kept, zt_done, act_own, t_done, sp_done,
         sum_done, tri_done, a_done, v_used, o_row, o_turned, dve_own, q_ready) = sems(
            ctx, nc, "sa", "zeroed", "kn_in", "vn_in", "k_turned", "act_kept", "dve_kept", "z_done", "z_kept",
            "zt_done", "act_own", "t_done", "sp_done", "sum_done", "tri_done", "a_done", "v_used", "o_row",
            "o_turned", "dve_own", "q_ready")
        k_in = sems(ctx, nc, "sa", *[f"k_in{j}" for j in range(4)])
        v_in = sems(ctx, nc, "sa", *[f"v_in{j}" for j in range(8)])
        block = ctx.enter_context(nc.Block())
        UNITS = 9
        TURNS = 2 + 8 * 8
        Z, ZT, OA, OT = k.ps[3], k.ps[4], k.ps[5], k.ps[6]
        WIDTH = [P] + [512] * 8
        NPG = [1] + [4] * 8
        JOB = [0] + [2 + 8 * u for u in range(8)]
        npages = a["cache_k"].shape[0]

        @block.sync
        def _(sp):
            kc = a["cache_k"].rearrange("n p h d -> n p (h d)")
            vc = a["cache_v"].rearrange("n p h d -> n p (h d)")
            kn = a["k_sample"].rearrange("b t h d -> b t (h d)")
            vn = a["v_sample"].rearrange("b t h d -> b t (h d)")
            sp.wait_ge(zeroed, 2)
            with sp.Fori(0, DB) as b:
                sp.wait_ge(k_turned, b * TURNS + 2)
                sp.dma_start(k_new[0:DS, :], kn[bass.ds(b, 1), :, :].rearrange("b t n -> (b t) n")).then_inc(kn_in, 16)
                sp.wait_ge(v_used, b * UNITS + 1)
                sp.dma_start(v_new[0:DS, :], vn[bass.ds(b, 1), :, :].rearrange("b t n -> (b t) n")).then_inc(vn_in, 16)
                for u in range(1, UNITS):
                    for g in range(4):
                        n = 4 * (u - 1) + g
                        slot = n % 8
                        page = sp.value_load(k.pages[0:1, bass.ds(b * PAGES + (PAGES - 1 - n), 1)],
                                             min_val=0, max_val=npages - 1)
                        sp.wait_ge(k_turned, b * TURNS + 2 * ((27 if u > 1 else 26) + 4 * u + g))
                        sp.dma_start(k_page[:, g, :], kc[bass.ds(page, 1), :, :].rearrange("n p d -> (n p) d")
                                     ).then_inc(k_in[g], 16)
                        sp.wait_ge(v_used, b * UNITS + (u + 8 if u > 2 else u + 7))
                        sp.dma_start(v_page[:, slot, :], vc[bass.ds(page, 1), :, :].rearrange("n p d -> (n p) d")
                                     ).then_inc(v_in[slot], 16)

        @block.gpsimd
        def _(pool):
            pool.memset(k_new[:, :], 0.0).then_inc(zeroed, 1)
            pool.memset(v_new[:, :], 0.0).then_inc(zeroed, 1)

        def keep_turned(eng, copy, mine, b, u, kept):
            for g in range(NPG[u]):
                for h in range(2):
                    job = JOB[u] + 2 * g + h
                    if job % 2 != mine:
                        continue
                    eng.wait_ge(k_turned, b * TURNS + (TURNS + job + 1))
                    eng.wait_ge(z_done, b * UNITS + (u + 1))
                    copy(k_t[:, 4 * h:4 * h + 4, g * P:(g + 1) * P],
                         k.ps[job % 3][:, :].rearrange("p (c n) -> p c n", c=4)).then_inc(kept, 1)

        @block.scalar
        def _(act):
            act.preload_act_table_set("natural_log_exp_and_others")
            act.sem_inc(act_kept, 33)
            with act.Fori(0, DB) as b:
                def weights(u):
                    act.wait_ge(tri_done, b * UNITS + (u + 1))
                    act.activation(att[:, u % 2, 0:WIDTH[u]], ZT[:, 0:WIDTH[u]], ACT.Exp).then_inc(a_done, 1)
                for u in range(UNITS):
                    w = WIDTH[u]
                    keep_turned(act, lambda out, in_: act.activation(out, in_, ACT.Copy), 0, b, u, act_kept)
                    if u:
                        weights(u - 1)
                    act.wait_ge(zt_done, b * UNITS + (u + 2))
                    act.wait_ge(sp_done, b * UNITS + (u + 1))
                    act.activation(t[:, 0:w], ZT[:, 0:w], ACT.Abs).then_inc(act_own, 1)
                    act.wait_ge(act_own, b * (2 * UNITS) + (2 * u + 1))
                    act.activation(t[:, 0:w], t[:, 0:w], ACT.Exp, scale=-1.0).then_inc(act_own, 1)
                    act.wait_ge(act_own, b * (2 * UNITS) + (2 * u + 2))
                    act.activation(t[:, 0:w], t[:, 0:w], ACT.Ln, bias=1.0).then_inc(t_done, 1)
                weights(UNITS - 1)

        @block.vector
        def _(dve):
            own = Tally(dve, dve_own)
            dve.sem_inc(dve_kept, 33)
            dve.sem_inc(z_kept, 1)
            dve.sem_inc(sp_done, 1)
            dve.sem_inc(o_row, 1)
            own.do(dve.memset(q_tiles[:, :, :], 0.0))
            own.do(dve.memset(o_rows[:, :], 0.0))
            OWN = 3 + UNITS + 3 * 8 - 1 + 3
            with dve.Fori(0, DB) as b:
                own.base, own.k = b * OWN + 2, 0
                dve.wait_ge(z_done, b * UNITS + 1)
                for par in range(2):
                    for e in range(2):
                        half = slice(64 * par, 64 * par + 64)
                        c = 16 * e + 8 * par
                        ins = dve.tensor_copy(
                            q_tiles[half, :, :].rearrange("p (g e) c -> p g e c", e=2)[:, :, e, c:c + 8],
                            k.q_t[half, :, bass.ds(b * DS + TP, DS)].rearrange("p (g e) c -> p g e c", e=2)[:, :, e, :])
                        if par and e:
                            ins.then_inc(q_ready, 1)
                        else:
                            own.mark(ins)
                for u in range(UNITS):
                    w, n = WIDTH[u], NPG[u]
                    keep_turned(dve, dve.tensor_copy, 1, b, u, dve_kept)
                    dve.wait_ge(z_done, b * UNITS + (u + 2))
                    dve.wait_ge(zt_done, b * UNITS + (u + 1))
                    dve.tensor_scalar(z_rows[:, 0:w], Z[:, 0:w], k.bias_row[:, 0:1], None, ALU.add
                                      ).then_inc(z_kept, 1)
                    spu = spl[:, u % 2, 0:n, :].rearrange("p g c -> p (g c)")
                    dve.wait_ge(act_own, b * (2 * UNITS) + (2 * u + 1))
                    own.mark(dve.tensor_scalar(spu, ZT[:, 0:w], 0.0, None, ALU.max))
                    own.settle()
                    dve.wait_ge(t_done, b * UNITS + (u + 1))
                    dve.tensor_tensor(spu, spu, t[:, 0:w], ALU.add).then_inc(sp_done, 1)
                    dve.wait_ge(sp_done, b * UNITS + (u + 2))
                    if u == 0:
                        dve.tensor_copy(behind[:, 1, 0, :], spl[:, 0, 0, :]).then_inc(sum_done, 1)
                        dve.wait_ge(sum_done, b * UNITS + 1)
                        continue
                    for g in range(1, 4):
                        ins = dve.tensor_tensor(behind[:, u % 2, g, :], behind[:, u % 2, g - 1, :],
                                                spl[:, u % 2, g - 1, :], ALU.add)
                        if g < 3:
                            own.do(ins)
                        else:
                            ins.then_inc(sum_done, 1)
                            dve.wait_ge(sum_done, b * UNITS + (u + 1))
                    if u < UNITS - 1:
                        own.do(dve.tensor_tensor(behind[:, (u + 1) % 2, 0, :], behind[:, u % 2, 3, :],
                                                 spl[:, u % 2, 3, :], ALU.add))
                dve.wait_ge(v_used, b * UNITS + 2 * UNITS)
                own.do(dve.tensor_tensor(o_part[:, :, :], OA[:, 0:4 * HD].rearrange("p (h d) -> p h d", h=4),
                                         over(k.block_of[:, :], HD), ALU.mult))
                dve.tensor_reduce(o_rows[:, 0:HD], o_part[:, :, :].rearrange("p h d -> p d h"), AX.X, ALU.add
                                  ).then_inc(o_row, 1)
                dve.wait_ge(o_turned, b + 1)
                for par in range(2):
                    own.mark(dve.tensor_copy(
                        k.o_s[64 * par:64 * par + 64, :, bass.ds(b * DS, DS)],
                        OT[0:64, 0:P].rearrange("p (c r q) -> p c r q", r=2, q=DS)[:, :, par, :]))
                own.settle()
                assert own.k == OWN, own.k

        @block.tensor
        def _(pe):
            pe.sem_inc(k_turned, TURNS)
            pe.sem_inc(z_done, 1)
            pe.sem_inc(zt_done, 1)
            pe.sem_inc(v_used, UNITS)
            with pe.Fori(0, DB) as b:
                def turn_keys(u):
                    for g in range(NPG[u]):
                        for h in range(2):
                            job = JOB[u] + 2 * g + h
                            if h == 0:
                                if u:
                                    pe.wait_ge(k_in[g], b * 128 + 16 * u)
                                else:
                                    pe.wait_ge(kn_in, b * 16 + 16)
                            last_job = job - 3 if job >= 3 else job + TURNS - 3
                            kept = act_kept if last_job % 2 == 0 else dve_kept
                            pe.wait_ge(kept, b * 33 + (last_job // 2 + 1 + (33 if job >= 3 else 0)))
                            src = k_page[:, g, :] if u else k_new[:, :]
                            for c in range(4):
                                last = pe.transpose(k.ps[job % 3][:, c * P:(c + 1) * P],
                                                    src[:, (4 * h + c) * P:(4 * h + c + 1) * P], k.ident[:, :])
                            last.then_inc(k_turned, 1)

                def scores(u):
                    w = WIDTH[u]
                    pe.wait_ge(act_kept, b * 33 + (33 + 4 * u + 1))
                    pe.wait_ge(dve_kept, b * 33 + (33 + 4 * u + 1))
                    pe.wait_ge(z_kept, b * UNITS + (u + 1))
                    if u == 0:
                        pe.wait_ge(q_ready, b + 1)
                    for e in range(2):
                        for q in range(4):
                            last = pe.matmul(Z[32 * q:32 * q + 32, 0:w], q_tiles[:, 2 * q + e, :],
                                             k_t[:, 2 * q + e, 0:w], start=(e == 0), stop=(e == 1),
                                             tile_position=(0, 32 * q), skip_group_check=True)
                    last.then_inc(z_done, 1)

                def turn_scores(u):
                    pe.wait_ge(z_kept, b * UNITS + (u + 2))
                    if u:
                        pe.wait_ge(a_done, b * UNITS + u)
                    for g in range(NPG[u]):
                        last = pe.matmul(ZT[:, g * P:(g + 1) * P], z_rows[:, g * P:(g + 1) * P], k.ident[:, :],
                                         start=(g == 0), stop=False, is_transpose=True, skip_group_check=True)
                    if u == 0:
                        last = pe.matmul(ZT[:, 0:P], k.ident_b[:, :], k.mask_new[:, :], start=False, stop=False,
                                         skip_group_check=True)
                    last.then_inc(zt_done, 1)

                def subtract_sums(u):
                    w = WIDTH[u]
                    pe.wait_ge(sp_done, b * UNITS + (u + 2))
                    last = pe.matmul(ZT[:, 0:w], k.neg_tri[:, :], spl[:, u % 2, 0:NPG[u], :].rearrange("p g c -> p (g c)"),
                                     start=False, stop=(u == 0), skip_group_check=True)
                    if u:
                        pe.wait_ge(sum_done, b * UNITS + (u + 1))
                        last = pe.matmul(ZT[:, 0:w], k.neg_ones[:, :], behind[:, u % 2, :, :].rearrange("p g c -> p (g c)"),
                                         start=False, stop=True, skip_group_check=True)
                    last.then_inc(tri_done, 1)

                def values(u):
                    pe.wait_ge(a_done, b * UNITS + (u + 1))
                    if u == 0:
                        pe.wait_ge(vn_in, b * 16 + 16)
                        pe.wait_ge(o_row, b + 1)
                    for g in range(NPG[u]):
                        if u:
                            slot = 4 * ((u - 1) % 2) + g
                            pe.wait_ge(v_in[slot], b * 64 + 16 * ((u - 1) // 2 + 1))
                        v = v_page[:, slot, :] if u else v_new[:, :]
                        for q in range(4):
                            last = pe.matmul(OA[32 * q:32 * q + 32, 0:4 * HD],
                                             att[:, u % 2, g * P + 32 * q:g * P + 32 * q + 32],
                                             v[:, 256 * q:256 * q + 256], start=(u == 0), stop=(u == 8 and g == 3),
                                             tile_position=(0, 32 * q), skip_group_check=True)
                    last.then_inc(v_used, 1)

                for u in range(UNITS):
                    turn_keys(u)
                    if u:
                        subtract_sums(u - 1)
                    scores(u)
                    if u:
                        values(u - 1)
                    turn_scores(u)
                subtract_sums(UNITS - 1)
                values(UNITS - 1)
                pe.wait_ge(o_row, b + 2)
                pe.transpose(OT[:, 0:P], o_rows[:, :], k.ident[:, :]).then_inc(o_turned, 1)


def attend_prompt(nc, k, a):
    with ExitStack() as ctx:
        o = k.WORK_AT
        k_rows = k.at("pa_k", [P, 2, 8, P], F32, o)
        v_rows = k.at("pa_v", [P, 2, 8, P], F32, o + 8192)
        k_t = k.at("pa_kt", [P, 2, TP], F32, o + 16384)
        q_s = k.at("pa_q", [P, 2, TP], F32, o + 24576)
        t = k.at("pa_t", [P, 2, 512], F32, o + 32768)
        spl = k.at("pa_sp", [P, 4, 512], F32, o + 36864)
        att = k.at("pa_a", [P, 3, 512], F32, o + 45056)
        behind = k.at("pa_behind", [P, 2, 3, 512], F32, o + 51200)
        bias = k.at("pa_bias", [P, 4], F32, o + 63488)
        (z_done, act_own, t_done, sp_done, tri_done, a_done, pv_done, dve_own, k_turned, k_kept, q_ready,
         o_kept) = sems(ctx, nc, "pa", "z_done", "act_own", "t_done", "sp_done", "tri_done", "a_done", "pv_done",
                        "dve_own", "k_turned", "k_kept", "q_ready", "o_kept")
        kv_in = sems(ctx, nc, "pa", "kv_in0", "kv_in1")
        block = ctx.enter_context(nc.Block())
        NT = 48

        class Tile:
            pass
        tiles = []
        for pp in range(2):
            for half in range(2):
                last_j = 4 * half + 3
                for n, j in enumerate(range(last_j, -1, -1)):
                    for head in range(2):
                        x = Tile()
                        x.pp, x.half, x.j, x.head, x.n = pp, half, j, head, n
                        x.q0 = max(P * j, 512 * half)
                        x.lo = x.q0 - 512 * half
                        x.w = 512 - x.lo
                        x.diag = P * j >= 512 * half
                        x.first, x.last = n == 0, j == 0
                        x.carry = P if x.diag else 0
                        x.acc = k.ps[4 + (2 * pp + half) % 2]
                        x.slot = len(tiles) // 2 % 3
                        tiles.append(x)
        ends = {i: x for i, x in enumerate(tiles) if x.last and x.head == 1}

        @block.sync
        def _(sp):
            kp = a["k_prompt"][0].rearrange("(j p) h d -> p j (h d)", p=P)
            vp = a["v_prompt"][0].rearrange("(j p) h d -> p j (h d)", p=P)
            with sp.Fori(0, 4) as i:
                for pp in range(2):
                    sp.wait_ge(pv_done, i * NT + 24 * (pp + 1))
                    cols = bass.ds((i * 2 + pp) * P, P)
                    sp.dma_start(k_rows[:, pp, :, :], kp[:, :, cols]).then_inc(kv_in[pp], 16)
                    sp.dma_start(v_rows[:, pp, :, :], vp[:, :, cols]).then_inc(kv_in[pp], 16)

        @block.scalar
        def _(act):
            act.preload_act_table_set("natural_log_exp_and_others")
            with act.Fori(0, 4) as i:
                for pp in range(2):
                    for h in range(2):
                        act.wait_ge(k_turned, i * 4 + (2 * pp + h + 1))
                        act.wait_ge(z_done, i * NT + 24 * (pp + 1))
                        act.activation(k_t[:, pp, 512 * h:512 * h + 512], k.ps[6 + h][:, :], ACT.Copy
                                       ).then_inc(k_kept, 1)
                act.wait_ge(q_ready, i + 1)
                for n in range(NT + 2):
                    if n < NT:
                        x = tiles[n]
                        tt, zz = t[:, n % 2, 0:x.w], k.ps[n % 4][:, 0:x.w]
                        b = bias[:, 2 * x.pp + x.head:2 * x.pp + x.head + 1]
                        act.wait_ge(z_done, i * NT + (NT + n + 1))
                        act.wait_ge(sp_done, i * NT + (n + 1))
                        act.activation(tt, zz, ACT.Abs, bias=b).then_inc(act_own, 1)
                        act.wait_ge(act_own, i * (2 * NT) + (2 * n + 1))
                        act.activation(tt, tt, ACT.Exp, scale=-1.0).then_inc(act_own, 1)
                        act.wait_ge(act_own, i * (2 * NT) + (2 * n + 2))
                        act.activation(tt, tt, ACT.Ln, bias=1.0).then_inc(t_done, 1)
                    m = n - 2
                    if m >= 0:
                        x = tiles[m]
                        act.wait_ge(tri_done, i * NT + (4 + m + 1))
                        act.wait_ge(pv_done, i * NT + (NT + m - 2))
                        act.activation(att[:, m % 3, 0:x.w], k.ps[m % 4][:, 0:x.w], ACT.Exp,
                                       bias=bias[:, 2 * x.pp + x.head:2 * x.pp + x.head + 1]).then_inc(a_done, 1)

        @block.vector
        def _(dve):
            own = Tally(dve, dve_own)
            dve.sem_inc(sp_done, 2)
            dve.sem_inc(o_kept, 2)
            own.do(dve.tensor_copy(k.hi[:, :, TP:T], k.o_s[:, :, :]))
            own.do(dve.tensor_tensor(k.lo[:, :, TP:T], k.o_s[:, :, :], k.hi[:, :, TP:T].bitcast(F32), ALU.subtract))
            before = own.k
            OWN = 2 + sum(1 + (0 if x.last else 2 if x.diag and not x.first else 1) for x in tiles) + 4
            with dve.Fori(0, 4) as i:
                own.base, own.k = i * OWN + before, 0
                dve.wait_ge(z_done, i * NT + NT)
                dve.wait_ge(a_done, i * NT + 4)
                own.mark(dve.tensor_copy(bias[:, :], k.bias_all[:, bass.ds(i * 4, 4)]))
                own.mark(dve.tensor_copy(q_s[:, 0, :], k.q_t[:, bass.ds(i * 2, 1), 0:TP].rearrange("p c n -> p (c n)")))
                dve.tensor_copy(q_s[:, 1, :], k.q_t[:, bass.ds(i * 2 + 1, 1), 0:TP].rearrange("p c n -> p (c n)")
                                ).then_inc(q_ready, 1)
                dve.wait_ge(q_ready, i + 1)

                def keep_output(x):
                    dve.wait_ge(pv_done, i * NT + (NT + tiles.index(x) + 1))
                    cols = slice(512 * x.half, 512 * x.half + 512)
                    hi = k.hi[:, bass.ds(i * 2 + x.pp, 1), cols].rearrange("p c n -> p (c n)")
                    lo = k.lo[:, bass.ds(i * 2 + x.pp, 1), cols].rearrange("p c n -> p (c n)")
                    own.do(dve.tensor_copy(hi, x.acc[:, :]))
                    dve.tensor_tensor(lo, x.acc[:, :], hi.bitcast(F32), ALU.subtract).then_inc(o_kept, 1)

                for n in range(NT + 4):
                    if n < NT:
                        x = tiles[n]
                        s = spl[:, n % 4, 0:x.w]
                        dve.wait_ge(act_own, i * (2 * NT) + (2 * n + 1))
                        dve.wait_ge(tri_done, i * NT + (n + 1))
                        own.do(dve.tensor_scalar(s, k.ps[n % 4][:, 0:x.w],
                                                 bias[:, 2 * x.pp + x.head:2 * x.pp + x.head + 1], 0.0,
                                                 ALU.add, ALU.max))
                        dve.wait_ge(t_done, i * NT + (n + 1))
                        dve.tensor_tensor(s, s, t[:, n % 2, 0:x.w], ALU.add).then_inc(sp_done, 1)
                        if not x.last:
                            dve.wait_ge(sp_done, i * NT + (2 + n + 1))
                            b_in, b_out = behind[:, x.head, x.slot, :], behind[:, x.head, (x.slot + 1) % 3, :]
                            new = x.w if x.first else x.carry
                            if new:
                                own.mark(dve.tensor_copy(b_out[:, x.lo:x.lo + new], s[:, 0:new]))
                            if new < x.w:
                                own.mark(dve.tensor_tensor(b_out[:, x.lo + new:512], b_in[:, x.lo + new:512],
                                                           s[:, new:x.w], ALU.add))
                    if n - 4 in ends:
                        keep_output(ends[n - 4])
                assert own.k == OWN, (own.k, OWN)

        @block.tensor
        def _(pe):
            pe.sem_inc(pv_done, NT)
            pe.sem_inc(z_done, NT)
            pe.sem_inc(tri_done, 4)
            pe.sem_inc(a_done, 4)
            with pe.Fori(0, 4) as i:
                for pp in range(2):
                    pe.wait_ge(kv_in[pp], i * 32 + 32)
                    for h in range(2):
                        if pp:
                            pe.wait_ge(k_kept, i * 4 + (h + 1))
                        elif h == 0:
                            pe.wait_ge(a_done, i * NT + 4)
                        for c in range(4):
                            last = pe.transpose(k.ps[6 + h][:, c * P:(c + 1) * P], k_rows[:, pp, 4 * h + c, :],
                                                k.ident[:, :])
                        last.then_inc(k_turned, 1)
                pe.wait_ge(k_kept, i * 4 + 4)
                pe.wait_ge(q_ready, i + 1)
                for n in range(NT + 3):
                    if n < NT:
                        x = tiles[n]
                        rows = slice(64 * x.head, 64 * x.head + 64)
                        z = k.ps[n % 4]
                        pe.wait_ge(a_done, i * NT + (n + 1))
                        last = pe.matmul(z[:, 0:x.w], k_t[rows, x.pp, P * x.j:P * x.j + P],
                                         q_s[rows, x.pp, x.q0:x.q0 + x.w], start=True, stop=False,
                                         skip_group_check=True)
                        if x.diag:
                            last = pe.matmul(z[:, 0:P], k.ident_b[:, :], k.mask_diag[:, :], start=False, stop=False,
                                             skip_group_check=True)
                        last.then_inc(z_done, 1)
                    if 0 <= n - 2 < NT:
                        m = n - 2
                        x = tiles[m]
                        z = k.ps[m % 4]
                        pe.wait_ge(sp_done, i * NT + (2 + m + 1))
                        last = pe.matmul(z[:, 0:x.w], k.neg_tri[:, :], spl[:, m % 4, 0:x.w], start=False, stop=x.first,
                                         skip_group_check=True)
                        if not x.first:
                            last = pe.matmul(z[:, x.carry:x.w], k.neg_ones[:, :],
                                             behind[:, x.head, x.slot, x.lo + x.carry:512], start=False, stop=True,
                                             skip_group_check=True)
                        last.then_inc(tri_done, 1)
                    if 0 <= n - 3:
                        m = n - 3
                        x = tiles[m]
                        pe.wait_ge(a_done, i * NT + (4 + m + 1))
                        if x.first and x.head == 0:
                            pe.wait_ge(o_kept, i * 4 + (2 * x.pp + x.half + 1))
                        pe.matmul(x.acc[64 * x.head:64 * x.head + 64, x.lo:512],
                                  v_rows[:, x.pp, x.j, 64 * x.head:64 * x.head + 64], att[:, m % 3, 0:x.w],
                                  start=x.first, stop=x.last, skip_group_check=True).then_inc(pv_done, 1)


def store_y(nc, k, a):
    with ExitStack() as ctx:
        y_rows = k.at("y_rows", [P, 9, D], F32, k.HH_AT)
        turned, act_kept, dve_kept, stored = sems(ctx, nc, "y", "turned", "act_kept", "dve_kept", "stored")
        block = ctx.enter_context(nc.Block())
        JOBS = 18

        def keep(eng, copy, mine, kept):
            for j in range(mine, JOBS, 2):
                t, half = divmod(j, 2)
                rows = P if t < 8 else TS
                eng.wait_ge(turned, j + 1)
                copy(y_rows[0:rows, t, 512 * half:512 * half + 512], k.ps[j % 8][0:rows, :]).then_inc(kept, 1)

        @block.tensor
        def _(pe):
            for j in range(JOBS):
                t, half = divmod(j, 2)
                rows = P if t < 8 else TS
                if j >= 8:
                    pe.wait_ge(dve_kept if j % 2 else act_kept, (j - 8) // 2 + 1)
                for c in range(4):
                    last = pe.transpose(k.ps[j % 8][0:rows, c * P:(c + 1) * P],
                                        k.x_t[:, 4 * half + c, t * P:t * P + rows], k.ident[:, :])
                last.then_inc(turned, 1)

        @block.scalar
        def _(act):
            keep(act, lambda out, in_: act.activation(out, in_, ACT.Copy), 0, act_kept)

        @block.vector
        def _(dve):
            keep(dve, dve.tensor_copy, 1, dve_kept)

        @block.sync
        def _(sp):
            for t in range(9):
                sp.wait_ge(act_kept, t + 1)
                sp.wait_ge(dve_kept, t + 1)
                dst = a["y_prompt"][0, t * P:(t + 1) * P, :] if t < 8 else a["y_sample"].rearrange("b t d -> (b t) d")
                sp.dma_start(dst, y_rows[0:P if t < 8 else TS, t, :]).then_inc(stored, 16)
            sp.wait_ge(stored, 9 * 16)


def build(nc, a, upto=99):
    k = Kernel()
    base = -(-nc.sbuf_base // 64) * 64
    end = nc.sbuf_usable_end
    X_BYTES = NC * T * 4

    placed = {}

    def at(name, shape, dtype, offset):
        if name not in placed:
            placed[name] = nc.alloc_sbuf_tensor_at(name, shape, dtype, offset=offset)
        return placed[name]
    k.at = at
    k.HH_AT = base + X_BYTES
    k.F_AT = k.HH_AT + 2 * X_BYTES
    k.WORK_AT = k.F_AT + X_BYTES
    WORK = 65280
    k.x_t = at("x_t", [P, NC, T], F32, base)
    k.hi = at("hi", [P, NC, T], F32R, k.HH_AT)
    k.lo = at("lo", [P, NC, T], F32R, k.HH_AT + X_BYTES)
    k.q_t = at("q_t", [P, NC, T], F32, k.F_AT)
    place = [k.WORK_AT + WORK]

    def const(name, shape, dtype):
        n = 1
        for x in shape[1:]:
            n *= x
        n *= {F32: 4, I32: 4, BF16: 2}[dtype]
        got = at(name, shape, dtype, place[0])
        place[0] += -(-n // 64) * 64
        assert place[0] <= end, (name, place[0], end)
        return got
    k.ident = const("ident", [P, P], F32)
    k.mean_of = const("mean_of", [P, P], F32)
    k.neg_ones = const("neg_ones", [P, P], F32)
    k.neg_tri = const("neg_tri", [P, P], F32)
    k.ident_b = const("ident_b", [P, P], BF16)
    k.mask_diag = const("mask_diag", [P, P], BF16)
    k.mask_new = const("mask_new", [P, P], BF16)
    k.mod = [const(f"mod{i}", [P, 48, 9], F32) for i in range(2)]
    k.vec_t = const("vec_t", [P, 168], F32)
    k.bias_all = const("bias_all", [P, H], F32)
    k.head_of = const("head_of", [P, H], F32)
    k.block_of = const("block_of", [P, 4], F32)
    k.bias_row = const("bias_row", [P, 1], F32)
    k.inv_seen = const("inv_seen", [P, 16], F32)
    k.scratch = at("scratch", [P, P], F32, k.F_AT + 20480)
    k.o_s = at("o_s", [P, NC, TS], F32, k.WORK_AT + WORK - 64 - 1472 - 2048 + 1472)
    k.pages = at("pages", [1, DB * PAGES], I32, k.WORK_AT + WORK - 64 - 2048 - 1088)
    v = k.vec_t
    k.b_ada = [v[:, 0:48], v[:, 48:96]]
    k.ln_g = [[v[:, 96 + 16 * l + 8 * w:104 + 16 * l + 8 * w] for w in range(2)] for l in range(2)]
    k.ln_b = [[v[:, 128 + 16 * l + 8 * w:136 + 16 * l + 8 * w] for w in range(2)] for l in range(2)]
    k.pool_scale = v[:, 160:168]
    k.ps = [nc.alloc_psum_tensor(f"bank{i}", [P, 512], F32) for i in range(8)]

    steps = [
        lambda: setup(nc, k, a),
        lambda: pool_mixer(nc, k, a),
        lambda: norm(nc, k, "n00", 0, 0, (0, 4, 3)),
        lambda: mlp(nc, k, "m0", 0, a["w_up"], a["w_down"]),
        lambda: norm(nc, k, "n01", 0, 1, "x"),
        lambda: keys_values(nc, k, a),
        lambda: modulate(nc, k, "h1", 1, 1, 0),
        lambda: project(nc, k, "q", a["w_q"], True),
        lambda: attend_sample(nc, k, a),
        lambda: attend_prompt(nc, k, a),
        lambda: project(nc, k, "wo", a["w_o"], False),
        lambda: norm(nc, k, "n10", 1, 0, (1, 4, 3)),
        lambda: mlp(nc, k, "m1", 1, a["w_up"], a["w_down"]),
        lambda: norm(nc, k, "n11", 1, 1, None),
        lambda: store_y(nc, k, a),
    ]
    for step in steps[:upto] if isinstance(upto, int) else [steps[n] for n in upto]:
        step()


INS = ["x_prompt", "x_sample", "cache_k", "cache_v", "state_pool", "page_table", "c_prompt", "c_sample", "w_ada",
       "b_ada", "ln_g", "ln_b", "w_pool", "pool_scale", "w_up", "w_down", "w_kv", "w_q", "w_o", "b_break"]
OUTS = {
    "y_prompt": (1, TP, D), "y_sample": (DB, DS, D), "k_prompt": (1, TP, H, HD), "v_prompt": (1, TP, H, HD),
    "pool_prompt": (1, 1, HIST, D), "k_sample": (DB, DS, H, HD), "v_sample": (DB, DS, H, HD),
    "pool_sample": (1, DB, HIST, D),
}


def kernel(**inputs):
    import numpy as np
    import concourse.bacc as bacc
    from concourse.bass_utils import run_bass_kernel_spmd

    nc = bacc.Bacc("TRN2", target_bir_lowering=False, num_devices=1)
    arrays, aps = {}, {}
    for name in INS:
        x = np.ascontiguousarray(inputs[name])
        arrays[f"in_{name}"] = x
        aps[name] = nc.dram_tensor(f"in_{name}", x.shape, mybir.dt.from_np(x.dtype), kind="ExternalInput").ap()
    for name, shape in OUTS.items():
        aps[name] = nc.dram_tensor(f"out_{name}", shape, F32, kind="ExternalOutput").ap()
    build(nc, aps)
    r = run_bass_kernel_spmd(nc, [arrays], core_ids=[0])
    return tuple(r.results[0][f"out_{name}"] for name in OUTS)
```

```python
from contextlib import ExitStack

import concourse.bass as bass
from concourse import mybir

ALU = mybir.AluOpType
ACT = mybir.ActivationFunctionType
AX = mybir.AxisListType
F32, F32R, BF16, I32 = mybir.dt.float32, mybir.dt.float32r, mybir.dt.bfloat16, mybir.dt.int32

P = 128
D = 1024
NC = D // P
TP = 1024
DB, DS = 8, 8
TS = DB * DS
T = TP + TS
WIN = (2, 4, 8, 16)
HIST = 15
H, HD = 16, 64
DFF = 4096
PAGES = 32
PIECES = [(0, 364), (364, 364), (728, 360)]
LASTP = TP - 728
ALPHA = 4.0 ** 0.25
EPS = 1e-5 / ALPHA ** 2
MASKED = -1e30


class Kernel:
    pass


def sems(ctx, nc, phase, *names):
    got = [nc.alloc_semaphore(f"{phase}_{n}") for n in names]
    ctx.callback(retire, nc, got)
    return got


def retire(nc, got):
    nc.clear_and_free_semaphores(got)
    nc.all_engine_barrier()


class Tally:

    def __init__(self, eng, sem):
        self.eng, self.sem, self.base, self.k = eng, sem, 0, 0

    def mark(self, ins):
        ins.then_inc(self.sem, 1)
        self.k += 1

    def settle(self):
        if isinstance(self.base, int) and self.base + self.k == 0:
            return
        self.eng.wait_ge(self.sem, self.base + self.k)

    def do(self, ins):
        self.mark(ins)
        self.settle()


def over(ap, n):
    return ap.unsqueeze(len(ap.shape)).to_broadcast(list(ap.shape) + [n])


def three(pe, out, w_hi, w_lo, x_hi, x_lo, start, stop):
    pe.matmul(out, w_hi, x_hi, start=start, stop=False, skip_group_check=True)
    pe.matmul(out, w_hi, x_lo, start=False, stop=False, skip_group_check=True)
    return pe.matmul(out, w_lo, x_hi, start=False, stop=stop, skip_group_check=True)


def take_modulation(dve, k, layer, n, turned):
    out = k.mod[layer][:, 16 * n:16 * n + 16, :].rearrange("p (g j) r -> p j g r", g=4)
    return dve.tensor_tensor(
        out, turned[:, :].rearrange("p (j g r) -> p j g r", j=4, g=4)[:, :, :, 0:9],
        over(k.b_ada[layer][:, 16 * n:16 * n + 16].rearrange("p (g j) -> p j g", g=4), 9), ALU.add)


def finish_modulation(dve, own, k, layer):
    m = k.mod[layer]
    for scale in (1, 4):
        own.mark(dve.tensor_scalar(m[:, 8 * scale:8 * scale + 8, :], m[:, 8 * scale:8 * scale + 8, :],
                                   1.0, None, ALU.add))
    for gate in (2, 5):
        own.mark(dve.tensor_scalar(m[:, 8 * gate:8 * gate + 8, :], m[:, 8 * gate:8 * gate + 8, :],
                                   1.0 / ALPHA, None, ALU.mult))
    own.settle()


def setup(nc, k, a):
    with ExitStack() as ctx:
        at = k.at
        x_rows = at("x_rows", [P, 9, D], F32, k.HH_AT)
        c_rows = at("c_rows", [P, D], F32, k.F_AT)
        c_e = at("c_e", [P, D], F32, k.F_AT + 4096)
        vec_rows = at("vec_rows", [P, 2, P], F32, k.F_AT + 8192)
        mod_rows = at("mod_rows", [P, 2, 512], F32, k.F_AT + 13312)
        w_raw = at("w_raw", [P, 4, 2048], F32, k.WORK_AT)
        ps = k.ps
        (x_in, c_in, v_in, made, x_turned, x_kept, x_free, c_done, c_turned, act_own, dve_own,
         ada_used, mod_kept, mod_turned, mod_out, v_turned, v_kept, b_in, z_set) = sems(
            ctx, nc, "set", "x_in", "c_in", "v_in", "made", "x_turned", "x_kept", "x_free", "c_done", "c_turned",
            "act_own", "dve_own", "ada_used", "mod_kept", "mod_turned", "mod_out", "v_turned",
            "v_kept", "b_in", "z_set")
        w_in = sems(ctx, nc, "set", "w_in0", "w_in1", "w_in2", "w_in3")
        block = ctx.enter_context(nc.Block())
        XJOBS = 18
        NIT = 3

        @block.sync
        def _(sp):
            sp.wait_ge(z_set, 2)
            sp.dma_start(c_rows[0:1, :], a["c_prompt"]).then_inc(c_in, 16)
            sp.dma_start(c_rows[1:9, :], a["c_sample"]).then_inc(c_in, 16)
            sp.dma_start(vec_rows[0:96, 0, :], a["b_ada"].rearrange("l (m p) -> (l m) p", p=P)).then_inc(v_in, 16)
            sp.dma_start(vec_rows[0:32, 1, :], a["ln_g"].rearrange("l s (m p) -> (l s m) p", p=P)).then_inc(v_in, 16)
            sp.dma_start(vec_rows[32:64, 1, :], a["ln_b"].rearrange("l s (m p) -> (l s m) p", p=P)).then_inc(v_in, 16)
            sp.dma_start(vec_rows[64:72, 1, :], a["pool_scale"].rearrange("l (m p) -> (l m) p", p=P)).then_inc(v_in, 16)
            sp.dma_start(k.bias_all[:, :], a["b_break"][0].partition_broadcast(P)).then_inc(b_in, 16)
            sp.dma_start(k.pages[:, :], a["page_table"].rearrange("b n -> (b n)").unsqueeze(0)).then_inc(b_in, 16)
            sp.dma_start(x_rows[:, 0:8, :], a["x_prompt"][0].rearrange("(t p) d -> p t d", p=P)).then_inc(x_in, 16)
            sp.dma_start(x_rows[0:TS, 8, :], a["x_sample"].rearrange("b t d -> (b t) d")).then_inc(x_in, 16)
            w = a["w_ada"][0].rearrange("(k p) n -> k p n", p=P)
            with sp.Fori(0, NIT) as it:
                for c in range(NC):
                    sp.wait_ge(ada_used, it * NC + (c + 1))
                    sp.dma_start(w_raw[:, c % 4, :], w[c, :, bass.ds(it * 2048, 2048)]).then_inc(w_in[c % 4], 16)
            sp.wait_ge(b_in, 32)

        @block.gpsimd
        def _(pool):
            def made_by(ins):
                ins.then_inc(made, 1)
                made_by.n += 1
                pool.wait_ge(made, made_by.n)
            made_by.n = 0
            pool.memset(c_rows[:, :], 0.0).then_inc(z_set, 1)
            pool.memset(vec_rows[:, :, :], 0.0).then_inc(z_set, 1)
            made_by(pool.memset(k.ident[:, :], 0.0))
            made_by(pool.affine_select(out=k.ident[:, :], in_=k.ident[:, :], compare_op=ALU.not_equal, fill=1.0,
                                       base=0, pattern=[[-1, P]], channel_multiplier=1))
            made_by(pool.memset(k.mean_of[:, :], 1.0 / D))
            made_by(pool.memset(k.zeros[:, :], 0.0))
            made_by(pool.memset(k.scratch[:, :], -1.0))
            made_by(pool.tensor_copy(k.neg_ones[:, :], k.scratch[:, :]))
            made_by(pool.affine_select(out=k.scratch[:, :], in_=k.scratch[:, :], compare_op=ALU.is_ge, fill=0.0,
                                       base=0, pattern=[[-1, P]], channel_multiplier=1))
            made_by(pool.tensor_copy(k.neg_tri[:, :], k.scratch[:, :]))
            made_by(pool.memset(k.scratch[:, :], 0.0))
            made_by(pool.affine_select(out=k.scratch[:, :], in_=k.scratch[:, :], compare_op=ALU.is_gt, fill=MASKED,
                                       base=0, pattern=[[1, P]], channel_multiplier=-1))
            made_by(pool.tensor_copy(k.mask_diag[:, :], k.scratch[:, :]))
            made_by(pool.memset(k.scratch[:, :], 0.0))
            s3 = k.scratch[:, 0:TS]
            made_by(pool.affine_select(out=s3, in_=s3, compare_op=ALU.is_gt, fill=MASKED, base=0,
                                       pattern=[[1, TS]], channel_multiplier=-1))
            s3 = s3.rearrange("p (b q) -> p b q", q=DS)
            made_by(pool.affine_select(out=s3, in_=s3, compare_op=ALU.is_ge, fill=MASKED, base=0,
                                       pattern=[[-DS, DB], [0, DS]], channel_multiplier=1))
            made_by(pool.tensor_copy(k.mask_new[:, :], k.scratch[:, 0:TS]))
            made_by(pool.tensor_copy(k.ident_b[:, :], k.ident[:, :]))
            made_by(pool.memset(k.head_of[:, :], 1.0))
            made_by(pool.affine_select(out=k.head_of[:, :], in_=k.head_of[:, :], compare_op=ALU.is_ge, fill=0.0,
                                       base=0, pattern=[[-DS, H]], channel_multiplier=1))
            made_by(pool.affine_select(out=k.head_of[:, :], in_=k.head_of[:, :], compare_op=ALU.is_ge, fill=0.0,
                                       base=DS - 1, pattern=[[DS, H]], channel_multiplier=-1))
            for t in range(HIST):
                made_by(pool.memset(k.inv_seen[:, t:t + 1], 1.0 / (t + 1)))

        MADE = 16 + HIST

        @block.scalar
        def _(act):
            own = Tally(act, act_own)
            act.wait_ge(c_in, 32)
            own.mark(act.activation(c_e[:, :], c_rows[:, :], ACT.Exp, scale=-1.0))
            for j in range(1, XJOBS, 2):
                t, half = j // 2, j % 2
                rows = P if t < 8 else TS
                act.wait_ge(x_turned, j + 1)
                act.activation(k.x_t[:, 4 * half:4 * half + 4, t * P:t * P + rows],
                               ps[j % 4][:, :].rearrange("p (c n) -> p c n", c=4)[:, :, 0:rows],
                               ACT.Copy).then_inc(x_free, 1)

        @block.vector
        def _(dve):
            own = Tally(dve, dve_own)
            own.do(dve.memset(k.c_t[:, :, :], 0.0))
            dve.wait_ge(act_own, 1)
            own.do(dve.tensor_scalar(c_e[:, :], c_e[:, :], 1.0, None, ALU.add))
            own.do(dve.reciprocal(c_e[:, :], c_e[:, :]))
            dve.tensor_tensor(c_rows[:, :], c_rows[:, :], c_e[:, :], ALU.mult).then_inc(c_done, 1)
            dve.wait_ge(c_turned, 1)
            dve.tensor_copy(k.c_t[:, :, 0:9], ps[4][:, 0:NC * 16].rearrange("p (c n) -> p c n", c=NC)[:, :, 0:9]
                            ).then_inc(c_done, 1)
            dve.wait_ge(v_turned, 1)
            own.do(dve.tensor_copy(k.vec_t[:, 0:96], ps[7][:, 256:352]))
            own.do(dve.tensor_copy(k.vec_t[:, 96:168], ps[7][:, 384:456]))
            for j in range(0, XJOBS, 2):
                t, half = j // 2, j % 2
                rows = P if t < 8 else TS
                dve.wait_ge(x_turned, j + 1)
                dve.tensor_copy(k.x_t[:, 4 * half:4 * half + 4, t * P:t * P + rows],
                                ps[j % 4][:, :].rearrange("p (c n) -> p c n", c=4)[:, :, 0:rows]).then_inc(x_kept, 1)
            for n in range(NIT):
                dve.wait_ge(ada_used, 4 + NC * (n + 1))
                dve.tensor_copy(mod_rows[:, n % 2, :], ps[5][:, :]).then_inc(mod_kept, 1)
                dve.wait_ge(mod_turned, n + 1)
                take_modulation(dve, k, 0, n, ps[6]).then_inc(mod_out, 1)
            dve.wait_ge(mod_out, NIT)
            finish_modulation(dve, own, k, 0)
            own.do(dve.tensor_tensor(k.mod[0][:, 16:24, :], k.mod[0][:, 16:24, :], over(k.pool_scale, 9), ALU.mult))
            dve.wait_ge(made, MADE)
            dve.wait_ge(b_in, 32)
            own.do(dve.tensor_reduce(k.block_of[:, :], k.head_of[:, :].rearrange("p (g h) -> p h g", g=4), AX.X, ALU.add))
            own.do(dve.tensor_tensor(k.head_of[:, :], k.head_of[:, :], k.bias_all[:, :], ALU.mult))
            own.do(dve.tensor_reduce(k.bias_row[:, :], k.head_of[:, :], AX.X, ALU.add))

        @block.tensor
        def _(pe):
            pe.sem_inc(ada_used, 4)
            pe.wait_ge(made, 2)
            pe.wait_ge(c_done, 1)
            for c in range(NC):
                last = pe.transpose(ps[4][:, 16 * c:16 * c + 9], c_rows[0:9, c * P:(c + 1) * P], k.ident[0:9, 0:9])
            last.then_inc(c_turned, 1)
            pe.wait_ge(v_in, 64)
            pe.transpose(ps[7][:, 256:352], vec_rows[0:96, 0, :], k.ident[0:96, 0:96])
            pe.transpose(ps[7][:, 384:456], vec_rows[0:72, 1, :], k.ident[0:72, 0:72]).then_inc(v_turned, 1)
            pe.wait_ge(x_in, 32)
            for j in range(XJOBS):
                t, half = j // 2, j % 2
                rows = P if t < 8 else TS
                if j >= 4:
                    pe.wait_ge(x_free if j % 2 else x_kept, (j - 4) // 2 + 1)
                for c in range(4):
                    last = pe.transpose(ps[j % 4][:, c * P:c * P + rows],
                                        x_rows[0:rows, t, (4 * half + c) * P:(4 * half + c + 1) * P],
                                        k.ident[0:rows, 0:rows])
                last.then_inc(x_turned, 1)
            pe.wait_ge(c_done, 2)
            for n in range(NIT):
                if n:
                    pe.wait_ge(mod_kept, n)
                for c in range(NC):
                    pe.wait_ge(w_in[c % 4], 16 * (2 * n + c // 4 + 1))
                    for g in range(4):
                        last = pe.matmul(ps[5][32 * g:32 * g + 32, :], k.c_t[:, c, :],
                                         w_raw[:, c % 4, 512 * g:512 * g + 512], start=(c == 0), stop=(c == NC - 1),
                                         tile_position=(0, 32 * g), skip_group_check=True)
                    last.then_inc(ada_used, 1)
                pe.wait_ge(mod_kept, n + 1)
                if n:
                    pe.wait_ge(mod_out, n)
                for j in range(4):
                    last = pe.transpose(ps[6][:, j * P:(j + 1) * P], mod_rows[:, n % 2, j * P:(j + 1) * P],
                                        k.ident[:, :])
                last.then_inc(mod_turned, 1)


def gated_add(dve, own, k, layer, gate, m, piece, psum, tmp, free):
    c0, w = PIECES[piece]
    wp = w if piece < 2 else LASTP
    g = k.mod[layer]
    if piece == 2:
        x = k.x_t[:, m, TP:T]
        t = tmp[:, 0:TS]
        own.settle()
        own.do(dve.tensor_tensor(t.rearrange("p (b t) -> p b t", b=DB),
                                 psum[:, wp:w].rearrange("p (b t) -> p b t", b=DB),
                                 over(g[:, 8 * gate + m, 1:9], DS), ALU.mult))
        own.mark(dve.tensor_tensor(x, x, t, ALU.add))
    x = k.x_t[:, m, c0:c0 + wp]
    dve.scalar_tensor_tensor(out=x, in0=psum[:, 0:wp], scalar=g[:, 8 * gate + m, 0:1], in1=x,
                             op0=ALU.mult, op1=ALU.add).then_inc(free, 1)


def modulate_sample(dve, own, k, layer, scale, shift, x, out):
    m = k.mod[layer]
    x4 = x.rearrange("p c (b t) -> p c b t", b=DB)
    o4 = out.rearrange("p c (b t) -> p c b t", b=DB)
    own.do(dve.tensor_tensor(o4, x4, over(m[:, 8 * scale:8 * scale + 8, 1:9], DS), ALU.mult))
    own.do(dve.tensor_tensor(o4, o4, over(m[:, 8 * shift:8 * shift + 8, 1:9], DS), ALU.add))


def norm(nc, k, name, layer, which, to):
    with ExitStack() as ctx:
        squares = k.at("norm_sq", [P, 3, NC, 364], F32, k.WORK_AT)
        h_full = k.at("norm_h", [P, NC, 364], F32, k.WORK_AT + 3 * NC * 364 * 4)
        inv_var = k.at("norm_inv", [P, 364], F32, k.WORK_AT + 4 * NC * 364 * 4)
        rstd = k.at("norm_rstd", [P, 364], F32, k.WORK_AT + 4 * NC * 364 * 4 + 1472)
        mu_done, centred, squared, var_done, dve_own, scaled, normed, h_done, h_split, inv_done, rstd_done = sems(
            ctx, nc, name, "mu_done", "centred", "squared", "var_done", "dve_own", "scaled", "normed", "h_done", "h_split",
            "inv_done", "rstd_done")
        block = ctx.enter_context(nc.Block())
        gain, bias = k.ln_g[layer][which], k.ln_b[layer][which]

        @block.tensor
        def _(pe):
            for s, (c0, w) in enumerate(PIECES):
                for m in range(NC):
                    last = pe.matmul(k.ps[s][:, 0:w], k.mean_of[:, :], k.x_t[:, m, c0:c0 + w],
                                     start=(m == 0), stop=(m == NC - 1))
                last.then_inc(mu_done, 1)
            for s, (c0, w) in enumerate(PIECES):
                pe.wait_ge(squared, s + 1)
                for m in range(NC):
                    last = pe.matmul(k.ps[3 + s][:, 0:w], k.mean_of[:, :], squares[:, s, m, 0:w],
                                     start=(m == 0), stop=(m == NC - 1))
                last.then_inc(var_done, 1)

        @block.vector
        def _(dve):
            own = Tally(dve, dve_own)
            for s, (c0, w) in enumerate(PIECES):
                dve.wait_ge(mu_done, s + 1)
                x = k.x_t[:, :, c0:c0 + w]
                dve.tensor_tensor(x, x, k.ps[s][:, 0:w].unsqueeze(1).to_broadcast([P, NC, w]),
                                  ALU.subtract).then_inc(centred, 1)
            dve.wait_ge(centred, 3)

            def scale_by_rstd(s):
                c0, w = PIECES[s]
                x = k.x_t[:, :, c0:c0 + w]
                dve.wait_ge(var_done, s + 1)
                own.do(dve.tensor_scalar(inv_var[:, 0:w], k.ps[3 + s][:, 0:w], EPS, None, ALU.add))
                dve.reciprocal(inv_var[:, 0:w], inv_var[:, 0:w]).then_inc(inv_done, 1)
                dve.wait_ge(rstd_done, s + 1)
                dve.wait_ge(squared, s + 1)
                dve.tensor_tensor(x, x, rstd[:, 0:w].unsqueeze(1).to_broadcast([P, NC, w]), ALU.mult).then_inc(scaled, 1)

            def halves(s):
                if to is None:
                    return
                c0, w = PIECES[s]
                hi, lo = k.hi[:, :, c0:c0 + w], k.lo[:, :, c0:c0 + w]
                full = k.x_t[:, :, c0:c0 + w]
                dve.wait_ge(normed, s + 1)
                if to != "x":
                    full = h_full[:, :, 0:w]
                    if s == 2:
                        dve.wait_ge(h_split, 2)
                        modulate_sample(dve, own, k, *to, k.x_t[:, :, TP:T], h_full[:, :, LASTP:w])
                    dve.wait_ge(h_done, s + 1)
                own.do(dve.tensor_copy(hi, full))
                dve.tensor_tensor(lo, full, hi.bitcast(F32), ALU.subtract).then_inc(h_split, 1)

            scale_by_rstd(0)
            scale_by_rstd(1)
            halves(0)
            scale_by_rstd(2)
            halves(1)
            halves(2)

        @block.scalar
        def _(act):
            for s, (c0, w) in enumerate(PIECES):
                act.wait_ge(centred, s + 1)
                act.activation(squares[:, s, :, 0:w], k.x_t[:, :, c0:c0 + w], ACT.Square).then_inc(squared, 1)

            def root(s):
                w = PIECES[s][1]
                act.wait_ge(inv_done, s + 1)
                if s:
                    act.wait_ge(scaled, s)
                act.activation(rstd[:, 0:w], inv_var[:, 0:w], ACT.Sqrt).then_inc(rstd_done, 1)

            def affine(s, chunks):
                c0, w = PIECES[s]
                act.wait_ge(scaled, s + 1)
                for m in chunks:
                    last = act.activation(k.x_t[:, m, c0:c0 + w], k.x_t[:, m, c0:c0 + w], ACT.Identity,
                                          bias=bias[:, m:m + 1], scale=gain[:, m:m + 1])
                if NC - 1 in chunks:
                    last.then_inc(normed, 1)

            root(0)
            for s, (c0, w) in enumerate(PIECES):
                affine(s, range(0, 4))
                if s < 2:
                    root(s + 1)
                affine(s, range(4, NC))
                if to in (None, "x"):
                    continue
                wp = w if s < 2 else LASTP
                layer_, scale, shift = to
                act.wait_ge(normed, s + 1)
                if s:
                    act.wait_ge(h_split, s)
                for m in range(NC):
                    last = act.activation(h_full[:, m, 0:wp], k.x_t[:, m, c0:c0 + wp], ACT.Identity,
                                          bias=k.mod[layer_][:, 8 * shift + m, 0:1],
                                          scale=k.mod[layer_][:, 8 * scale + m, 0:1])
                last.then_inc(h_done, 1)


def pool_mixer(nc, k, a):
    with ExitStack() as ctx:
        o = k.WORK_AT
        HW = 16 + TP
        h_p = k.at("pm_hp", [P, 2, HW], F32, o)
        s_p = k.at("pm_sp", [P, 2, HW], F32, o + 2 * HW * 4)
        o += 4 * HW * 4
        h_s = k.at("pm_hs", [P, 2, DB, 24], F32, o)
        s_s = k.at("pm_ss", [P, 2, DB, 24], F32, o + 1536)
        d = k.at("pm_d", [P, T], F32, o + 3072)
        o += 3072 + T * 4
        w_raw = k.at("pm_wraw", [P, 4, 2, 256], F32, o)
        w_hi = k.at("pm_whi", [P, 4, 2, 256], F32R, o + 8192)
        w_lo = k.at("pm_wlo", [P, 4, 2, 256], F32R, o + 16384)
        o += 24576
        tail_p = k.at("pm_tp", [P, NC, HIST], F32, o)
        tail_s = k.at("pm_ts", [P, NC, TS], F32, o + 480)
        tmp = k.at("pm_tmp", [P, TS], F32, o + 480 + 2048)
        o += 480 + 2048 + 256
        hist = k.at("pm_hist", [P, D], F32, k.F_AT)
        out_p = k.at("pm_op", [P, D], F32, k.F_AT + 4096)
        out_s = k.at("pm_os", [P, D], F32, k.F_AT + 8192)
        mod_rows = k.at("pm_modrows", [P, 512], F32, k.F_AT + 13312)
        w_ada = k.at("pm_wada", [P, 4, 1024], F32, k.F_AT + 17408)
        (hist_in, w_in, hist_turned, h_done, h_used, dve_own, d_done, hi_done, whi_done, w_done, mixed, free,
         tails, turned, kept, stored, ada_used, mod_kept, mod_turned, mod_out) = sems(
            ctx, nc, "pm", "hist_in", "w_in", "hist_turned", "h_done", "h_used", "dve_own", "d_done", "hi_done",
            "whi_done", "w_done", "mixed", "free", "tails", "turned", "kept", "stored", "ada_used",
            "mod_kept", "mod_turned", "mod_out")
        ada_in = sems(ctx, nc, "pm", *[f"ada_in{j}" for j in range(4)])
        block = ctx.enter_context(nc.Block())
        ps = k.ps

        @block.sync
        def _(sp):
            sp.dma_start(hist[0:DB * HIST, :], a["state_pool"][0].rearrange("b r d -> (b r) d")).then_inc(hist_in, 16)
            sp.dma_start(w_raw[:, :, :, :], a["w_pool"][0].rearrange("g (c p) n -> p g c n", p=P)).then_inc(w_in, 16)
            sp.dma_start(a["pool_sample"][0, :, 0:HIST - DS, :], a["state_pool"][0, :, DS:HIST, :]).then_inc(stored, 16)
            w = a["w_ada"][1].rearrange("(k p) n -> k p n", p=P)
            with sp.Fori(0, 3) as it:
                for r in range(2 * NC):
                    sp.wait_ge(ada_used, it * (2 * NC) + (r + 1))
                    sp.dma_start(w_ada[:, r % 4, :], w[r // 2, :, bass.ds(it * 2048 + 1024 * (r % 2), 1024)]
                                 ).then_inc(ada_in[r % 4], 16)
            sp.wait_ge(kept, 2)
            sp.dma_start(a["pool_prompt"][0, 0], out_p[0:HIST, :]).then_inc(stored, 16)
            sp.wait_ge(kept, 4)
            sp.dma_start(a["pool_sample"][0, :, HIST - DS:HIST, :], out_s[0:TS, :]).then_inc(stored, 16)
            sp.wait_ge(stored, 48)

        @block.scalar
        def _(act):
            act.wait_ge(w_in, 16)
            act.activation(w_hi[:, :, :, :], w_raw[:, :, :, :], ACT.Copy).then_inc(whi_done, 1)
            for c in range(NC):
                if c >= 2:
                    act.wait_ge(h_used, c - 1)
                act.activation(h_p[:, c % 2, 16:HW], k.x_t[:, c, 0:TP], ACT.Identity,
                               bias=k.mod[0][:, c, 0:1], scale=k.mod[0][:, 8 + c, 0:1]).then_inc(h_done, 1)

        @block.vector
        def _(dve):
            own = Tally(dve, dve_own)
            own.mark(dve.memset(h_p[:, :, 0:16], 0.0))
            own.do(dve.memset(h_s[:, :, :, 0:1], 0.0))
            dve.wait_ge(whi_done, 1)
            dve.tensor_tensor(w_lo[:, :, :, :], w_raw[:, :, :, :], w_hi[:, :, :, :].bitcast(F32),
                              ALU.subtract).then_inc(w_done, 1)
            dve.wait_ge(hist_turned, 1)

            def chunk(c):
                win = WIN[c // 2]
                b = c % 2
                hs, hp = h_s[:, b, :, :], h_p[:, b, :]
                x = k.x_t[:, c, TP:T].rearrange("p (b t) -> p b t", b=DB)
                own.mark(dve.tensor_copy(hs[:, :, 1:16],
                                         ps[6 + c // 4][:, (c % 4) * P:(c % 4) * P + DB * HIST]
                                         .rearrange("p (b r) -> p b r", b=DB)))
                own.do(dve.tensor_tensor(hs[:, :, 16:24], x, over(k.mod[0][:, 8 + c, 1:9], DS), ALU.mult))
                own.do(dve.tensor_tensor(hs[:, :, 16:24], hs[:, :, 16:24], over(k.mod[0][:, c, 1:9], DS), ALU.add))
                own.mark(dve.tensor_copy(tail_s[:, c, :].rearrange("p (b t) -> p b t", b=DB), hs[:, :, 16:24]))
                dve.wait_ge(h_done, c + 1)
                own.mark(dve.tensor_copy(tail_p[:, c, :], hp[:, HW - HIST:HW]))
                src_p, src_s, step, lo, n = hp, hs, 1, 1, 0
                while step < win:
                    dst_p, dst_s = s_p[:, n % 2, :], s_s[:, n % 2, :, :]
                    own.mark(dve.tensor_tensor(dst_p[:, lo:HW], src_p[:, lo:HW], src_p[:, lo - step:HW - step], ALU.add))
                    own.do(dve.tensor_tensor(dst_s[:, :, lo:24], src_s[:, :, lo:24], src_s[:, :, lo - step:24 - step],
                                             ALU.add))
                    src_p, src_s, step, n = dst_p, dst_s, 2 * step, n + 1
                    lo += step
                if c:
                    dve.wait_ge(hi_done, c)
                own.mark(dve.scalar_tensor_tensor(out=d[:, win - 1:TP], in0=src_p[:, 15 + win:HW], scalar=1.0 / win,
                                                  in1=hp[:, 15 + win:HW], op0=ALU.mult, op1=ALU.subtract))
                own.mark(dve.scalar_tensor_tensor(out=d[:, TP:T].rearrange("p (b t) -> p b t", b=DB),
                                                  in0=src_s[:, :, 16:24], scalar=1.0 / win, in1=hs[:, :, 16:24],
                                                  op0=ALU.mult, op1=ALU.subtract))
                own.do(dve.tensor_tensor(d[:, 0:win - 1], src_p[:, 16:15 + win], k.inv_seen[:, 0:win - 1], ALU.mult))
                own.do(dve.tensor_tensor(d[:, 0:win - 1], d[:, 0:win - 1], hp[:, 16:15 + win], ALU.subtract))
                dve.tensor_copy(k.hi[:, c, :], d[:, :]).then_inc(h_used, 1)
                dve.wait_ge(h_used, c + 1)
                dve.tensor_tensor(k.lo[:, c, :], d[:, :], k.hi[:, c, :].bitcast(F32), ALU.subtract).then_inc(hi_done, 1)

            for c in range(NC):
                chunk(c)
                if c % 2:
                    n = c // 2
                    if n < 3:
                        dve.wait_ge(ada_used, 4 + 2 * NC * (n + 1))
                        dve.tensor_copy(mod_rows[:, :], ps[4][:, :]).then_inc(mod_kept, 1)
                    for j in range(6 * (c // 2), 6 * (c // 2) + 6):
                        m, s = divmod(j, 3)
                        dve.wait_ge(mixed, j + 1)
                        gated_add(dve, own, k, 0, 2, m, s, ps[j % 4], tmp, free)
                    if n < 3:
                        dve.wait_ge(mod_turned, n + 1)
                        take_modulation(dve, k, 1, n, ps[5]).then_inc(mod_out, 1)
            dve.wait_ge(mod_out, 3)
            finish_modulation(dve, own, k, 1)
            own.settle()
            dve.tensor_copy(tmp[:, 0:1], tail_s[:, 0, 0:1]).then_inc(tails, 1)
            for half in range(2):
                dve.wait_ge(turned, half + 1)
                dve.tensor_copy(out_p[0:HIST, 512 * half:512 * half + 512], ps[4 + half][0:HIST, :]).then_inc(kept, 1)
            for half in range(2):
                dve.wait_ge(turned, half + 3)
                dve.tensor_copy(out_s[0:TS, 512 * half:512 * half + 512], ps[6 + half][0:TS, :]).then_inc(kept, 1)

        @block.tensor
        def _(pe):
            pe.wait_ge(hist_in, 16)
            for c in range(NC):
                last = pe.transpose(ps[6 + c // 4][:, (c % 4) * P:(c % 4) * P + DB * HIST],
                                    hist[0:DB * HIST, c * P:(c + 1) * P], k.ident[0:DB * HIST, 0:DB * HIST])
            last.then_inc(hist_turned, 1)
            pe.wait_ge(w_done, 1)
            pe.sem_inc(ada_used, 4)

            def modulation(n):
                if n:
                    pe.wait_ge(mod_kept, n)
                for r in range(2 * NC):
                    pe.wait_ge(ada_in[r % 4], 16 * (4 * n + r // 4 + 1))
                    for g in range(2 * (r % 2), 2 * (r % 2) + 2):
                        last = pe.matmul(ps[4][32 * g:32 * g + 32, :], k.c_t[:, r // 2, :],
                                         w_ada[:, r % 4, 512 * (g % 2):512 * (g % 2) + 512], start=(r < 2),
                                         stop=(r >= 2 * NC - 2), tile_position=(0, 32 * g), skip_group_check=True)
                    last.then_inc(ada_used, 1)

            def turn_modulation(n):
                pe.wait_ge(mod_kept, n + 1)
                if n:
                    pe.wait_ge(mod_out, n)
                for j in range(4):
                    last = pe.transpose(ps[5][:, j * P:(j + 1) * P], mod_rows[:, j * P:(j + 1) * P], k.ident[:, :])
                last.then_inc(mod_turned, 1)

            for j in range(24):
                m, s = divmod(j, 3)
                g = m // 2
                if j % 6 == 0 and g < 3:
                    modulation(g)
                c0, w = PIECES[s]
                pe.wait_ge(hi_done, 2 * g + 2)
                if j >= 4:
                    pe.wait_ge(free, j - 3)
                for c in range(2):
                    col = (m % 2) * P
                    last = three(pe, ps[j % 4][:, 0:w], w_hi[:, g, c, col:col + P], w_lo[:, g, c, col:col + P],
                                 k.hi[:, 2 * g + c, c0:c0 + w], k.lo[:, 2 * g + c, c0:c0 + w], c == 0, c == 1)
                last.then_inc(mixed, 1)
                if j % 6 == 5 and g < 3:
                    turn_modulation(g)
            pe.wait_ge(tails, 1)
            pe.wait_ge(mod_out, 3)
            for rows, tail, bank in ((HIST, tail_p, 4), (TS, tail_s, 6)):
                for c in range(NC):
                    last = pe.transpose(ps[bank + c // 4][0:rows, (c % 4) * P:(c % 4 + 1) * P], tail[:, c, :],
                                        k.ident[:, :])
                    if c % 4 == 3:
                        last.then_inc(turned, 1)


def mlp(nc, k, name, layer, w_up, w_down):
    NB, FC, JOBS, BANKS, TILES = DFF // 512, 4, 36, 6, 8
    with ExitStack() as ctx:
        o = k.WORK_AT
        raw = k.at("mlp_raw", [P, 2, D], F32, o)
        up_hi = k.at("mlp_uphi", [P, 2, NC, P], F32R, o + 8192)
        up_lo = k.at("mlp_uplo", [P, 2, NC, P], F32R, o + 16384)
        dn_hi = k.at("mlp_dnhi", [P, FC, D], F32R, o + 24576)
        dn_lo = k.at("mlp_dnlo", [P, FC, D], F32R, o + 40960)
        f = k.at("mlp_f", [P, 2, 364], F32, o + 57344)
        tmp = k.at("mlp_tmp", [P, TS], F32, o + 57344 + 2912)
        f_hi = k.at("mlp_fhi", [P, FC, T], F32R, k.F_AT)
        f_lo = k.at("mlp_flo", [P, FC, T], F32R, k.F_AT + FC * T * 4)
        w_hi_done, w_done, job_done, bank_free, dve_own = sems(
            ctx, nc, name, "w_hi_done", "w_done", "job_done", "bank_free", "dve_own")
        raw_in = sems(ctx, nc, name, "raw_in0", "raw_in1")
        block = ctx.enter_context(nc.Block())
        up = w_up[layer].rearrange("(k p) n -> p k n", p=P)
        down = w_down[layer]
        ORDER = [("down", 0), ("up", 2), ("down", 1), ("up", 3), ("down", 2), ("down", 3), ("next", 0), ("next", 1)]

        def split_target(kind, c):
            if kind == "down":
                return dn_hi[:, c, :], dn_lo[:, c, :]
            return (up_hi[:, c % 2, :, :].rearrange("p k n -> p (k n)"),
                    up_lo[:, c % 2, :, :].rearrange("p k n -> p (k n)"))

        @block.sync
        def _(sp):
            def load(n, slot, kind, c, i):
                sp.wait_ge(w_done, n + 1)
                if kind == "down":
                    src, dst = down[bass.ds((i * FC + c) * P, P), :], raw[:, slot, :]
                else:
                    src = up[:, :, bass.ds((i * FC + c) * P, P)]
                    dst = raw[:, slot, :].rearrange("p (k n) -> p k n", k=NC)
                sp.dma_start(dst, src).then_inc(raw_in[slot], 16)
            load(0, 0, "up", 0, 0)
            load(1, 1, "up", 1, 0)
            with sp.Fori(0, NB - 1) as i:
                for r, (kind, c) in enumerate(ORDER):
                    load(i * TILES + (2 + r), r % 2, kind, c, i + 1 if kind == "next" else i)
            for r, (kind, c) in enumerate(ORDER[:6]):
                load((NB - 1) * TILES + 2 + r, r % 2, kind, c, NB - 1)

        @block.scalar
        def _(act):
            def hi_half(i, r, kind, c):
                before = {"down": 0, "up": 3 * (c - 1), "next": 9 + 3 * (c % 2)}[kind]
                act.wait_ge(raw_in[r % 2], i * (TILES // 2 * 16) + 16 * ((2 + r) // 2 + 1))
                act.wait_ge(job_done, i * JOBS + (before + 1))
                act.activation(split_target(kind, c)[0], raw[:, r % 2, :], ACT.Copy).then_inc(w_hi_done, 1)
            for c in range(2):
                act.wait_ge(raw_in[c], 16)
                act.activation(split_target("up", c)[0], raw[:, c, :], ACT.Copy).then_inc(w_hi_done, 1)
            with act.Fori(0, NB - 1) as i:
                for r, (kind, c) in enumerate(ORDER):
                    hi_half(i, r, kind, c)
            for r, (kind, c) in enumerate(ORDER[:6]):
                hi_half(NB - 1, r, kind, c)

        @block.gpsimd
        def _(pool):
            def lo_half(n, slot, kind, c):
                hi, lo = split_target(kind, c)
                pool.wait_ge(w_hi_done, n + 1)
                pool.tensor_tensor(lo, raw[:, slot, :], hi.bitcast(F32), ALU.subtract).then_inc(w_done, 1)
            pool.sem_inc(w_done, 2)
            lo_half(0, 0, "up", 0)
            lo_half(1, 1, "up", 1)
            with pool.Fori(0, NB - 1) as i:
                for r, (kind, c) in enumerate(ORDER):
                    lo_half(i * TILES + (2 + r), r % 2, kind, c)
            for r, (kind, c) in enumerate(ORDER[:6]):
                lo_half((NB - 1) * TILES + 2 + r, r % 2, kind, c)

        @block.vector
        def _(dve):
            own = Tally(dve, dve_own)
            with dve.Fori(0, NB) as i:
                own.base, own.k = i * (36 + 16), 0
                for j in range(12):
                    c, s = divmod(j, 3)
                    c0, w = PIECES[s]
                    dve.wait_ge(job_done, i * JOBS + (j + 2))
                    u = k.ps[j % BANKS][:, 0:w]
                    ft = f[:, j % 2, 0:w]
                    own.do(dve.tensor_scalar(ft, u, 0.0, None, ALU.max))
                    own.do(dve.tensor_tensor(ft, ft, ft, ALU.mult))
                    hi = f_hi[:, c, c0:c0 + w]
                    own.do(dve.tensor_copy(hi, ft))
                    dve.tensor_tensor(f_lo[:, c, c0:c0 + w], ft, hi.bitcast(F32), ALU.subtract).then_inc(bank_free, 1)
                dve.wait_ge(bank_free, i * JOBS + (BANKS + 12))
                for j in range(12, JOBS):
                    s, m = divmod(j - 12, NC)
                    dve.wait_ge(job_done, i * JOBS + (j + 2))
                    gated_add(dve, own, k, layer, 5, m, s, k.ps[j % BANKS], tmp, bank_free)

        @block.tensor
        def _(pe):
            pe.sem_inc(bank_free, BANKS)
            pe.sem_inc(job_done, 1)
            with pe.Fori(0, NB) as i:
                for j in range(JOBS):
                    pe.wait_ge(bank_free, i * JOBS + (j + 1))
                    if j < 12:
                        c, s = divmod(j, 3)
                        c0, w = PIECES[s]
                        if s == 0:
                            pe.wait_ge(w_done, i * TILES + (2 + (1, 2, 4, 6)[c]))
                        for q in range(NC):
                            last = three(pe, k.ps[j % BANKS][:, 0:w], up_hi[:, c % 2, q, :], up_lo[:, c % 2, q, :],
                                         k.hi[:, q, c0:c0 + w], k.lo[:, q, c0:c0 + w], q == 0, q == NC - 1)
                    else:
                        s, m = divmod(j - 12, NC)
                        c0, w = PIECES[s]
                        if m == 0:
                            if s == 0:
                                pe.wait_ge(w_done, i * TILES + (2 + 8))
                            pe.wait_ge(bank_free, i * JOBS + (BANKS + 10 + s))
                        for q in range(FC):
                            last = three(pe, k.ps[j % BANKS][:, 0:w], dn_hi[:, q, m * P:(m + 1) * P],
                                         dn_lo[:, q, m * P:(m + 1) * P], f_hi[:, q, c0:c0 + w],
                                         f_lo[:, q, c0:c0 + w], q == 0, q == FC - 1)
                    last.then_inc(job_done, 1)


def keys_values(nc, k, a):
    NBLK, W, TILES, BANKS = 8, 256, 9, 6
    with ExitStack() as ctx:
        o = k.WORK_AT
        raw = k.at("kv_raw", [P, 2, NC, W], F32, o)
        w_hi = k.at("kv_hi", [P, 2, NC, W], F32R, o + 16384)
        w_lo = k.at("kv_lo", [P, 2, NC, W], F32R, o + 32768)
        stage = k.at("kv_stage", [P, BANKS, W], F32, o + 49152)
        w_hi_done, w_done, job_done, kept = sems(ctx, nc, "kv", "w_hi_done", "w_done", "job_done", "kept")
        raw_in = sems(ctx, nc, "kv", "raw_in0", "raw_in1")
        stored = sems(ctx, nc, "kv", *[f"stored{j}" for j in range(BANKS)])
        block = ctx.enter_context(nc.Block())
        w = a["w_kv"].rearrange("(k p) n -> p k n", p=P)

        @block.sync
        def _(sp):
            for j in range(BANKS):
                sp.sem_inc(stored[j], 16)
            for n in range(2):
                sp.dma_start(raw[:, n, :, :], w[:, :, n * W:(n + 1) * W]).then_inc(raw_in[n], 16)

            def blocks(kv, i, ahead):
                kp = (a["k_prompt"], a["v_prompt"])[kv][0].rearrange("t h d -> t (h d)")
                ks = (a["k_sample"], a["v_sample"])[kv].rearrange("b t h d -> (b t) (h d)")
                for n in range(2):
                    for t in range(TILES):
                        j = n * TILES + t
                        rows = P if t < 8 else TS
                        dst = kp[t * P:(t + 1) * P, :] if t < 8 else ks
                        sp.wait_ge(kept, i * 18 + (36 * kv + BANKS + j + 1))
                        sp.dma_start(dst[:, bass.ds((i * 2 + n) * W, W)], stage[0:rows, j % BANKS, :]
                                     ).then_inc(stored[j % BANKS], 16)
                    if ahead:
                        sp.wait_ge(w_done, i * 2 + (4 * kv + n + 3))
                        sp.dma_start(raw[:, n, :, :], w[:, :, bass.ds((i * 2 + (4 * kv + n + 2)) * W, W)]
                                     ).then_inc(raw_in[n], 16)
            with sp.Fori(0, 2) as i:
                blocks(0, i, True)
            blocks(1, 0, True)
            blocks(1, 1, False)
            for j in range(BANKS):
                sp.wait_ge(stored[j], 16 * (72 // BANKS + 1))

        @block.scalar
        def _(act):
            with act.Fori(0, 4) as i:
                for n in range(2):
                    act.wait_ge(raw_in[n], i * 16 + 16)
                    act.wait_ge(job_done, i * 18 + (n * 9 + 9))
                    act.activation(w_hi[:, n, :, :], raw[:, n, :, :], ACT.Copy).then_inc(w_hi_done, 1)

        @block.gpsimd
        def _(pool):
            pool.sem_inc(w_done, 2)
            with pool.Fori(0, 4) as i:
                for n in range(2):
                    pool.wait_ge(w_hi_done, i * 2 + (n + 1))
                    pool.tensor_tensor(w_lo[:, n, :, :], raw[:, n, :, :], w_hi[:, n, :, :].bitcast(F32),
                                       ALU.subtract).then_inc(w_done, 1)

        @block.vector
        def _(dve):
            with dve.Fori(0, 4) as i:
                for j in range(18):
                    rows = P if j % TILES < 8 else TS
                    dve.wait_ge(job_done, i * 18 + (18 + j + 1))
                    dve.wait_ge(stored[j % BANKS], i * 48 + 16 * (j // BANKS + 1))
                    dve.tensor_copy(stage[0:rows, j % BANKS, :], k.ps[j % BANKS][0:rows, 0:W]).then_inc(kept, 1)

        @block.tensor
        def _(pe):
            pe.sem_inc(job_done, 18)
            pe.sem_inc(kept, BANKS)
            with pe.Fori(0, 4) as i:
                for j in range(18):
                    n, t = divmod(j, TILES)
                    rows = P if t < 8 else TS
                    if t == 0:
                        pe.wait_ge(w_done, i * 2 + (2 + n + 1))
                    pe.wait_ge(kept, i * 18 + (j + 1))
                    for q in range(NC):
                        x_hi, x_lo = k.hi[:, q, t * P:t * P + rows], k.lo[:, q, t * P:t * P + rows]
                        last = three(pe, k.ps[j % BANKS][0:rows, 0:W], x_hi, x_lo, w_hi[:, n, q, :],
                                     w_lo[:, n, q, :], q == 0, q == NC - 1)
                    last.then_inc(job_done, 1)


def project(nc, k, name, w_dram, to_query):
    BANKS = 6
    with ExitStack() as ctx:
        o = k.WORK_AT
        raw = k.at("proj_raw", [P, 2, NC, P], F32, o)
        w_hi = k.at("proj_hi", [P, 2, NC, P], F32R, o + 8192)
        w_lo = k.at("proj_lo", [P, 2, NC, P], F32R, o + 16384)
        tmp = k.at("proj_tmp", [P, TS], F32, o + 24576)
        h_full = k.at("proj_h", [P, 2, NC, 364], F32, o + 24832)
        w_hi_done, w_done, job_done, bank_free, dve_own, h_done, h_split = sems(
            ctx, nc, name, "w_hi_done", "w_done", "job_done", "bank_free", "dve_own", "h_done", "h_split")
        raw_in = sems(ctx, nc, name, "raw_in0", "raw_in1")
        block = ctx.enter_context(nc.Block())
        w = w_dram[0].rearrange("(k p) n -> p k n", p=P)

        @block.sync
        def _(sp):
            with sp.Fori(0, 4) as i:
                for n in range(2):
                    sp.wait_ge(w_done, i * 2 + (n + 1))
                    sp.dma_start(raw[:, n, :, :], w[:, :, bass.ds((i * 2 + n) * P, P)]).then_inc(raw_in[n], 16)

        @block.scalar
        def _(act):
            def modulate(s):
                layer, scale, shift = to_query
                c0, w_ = PIECES[s]
                wp = w_ if s < 2 else LASTP
                if s >= 2:
                    act.wait_ge(h_split, s - 1)
                for m in range(NC):
                    last = act.activation(h_full[:, s % 2, m, 0:wp], k.x_t[:, m, c0:c0 + wp], ACT.Identity,
                                          bias=k.mod[layer][:, 8 * shift + m, 0:1],
                                          scale=k.mod[layer][:, 8 * scale + m, 0:1])
                last.then_inc(h_done, 1)

            for m in range(NC):
                act.wait_ge(raw_in[m % 2], 16 * (m // 2 + 1))
                act.wait_ge(job_done, 3 * m + 3)
                act.activation(w_hi[:, m % 2, :, :], raw[:, m % 2, :, :], ACT.Copy).then_inc(w_hi_done, 1)
                if to_query and m == 0:
                    modulate(0)
                if to_query and m == 1:
                    modulate(1)
                    modulate(2)

        @block.gpsimd
        def _(pool):
            pool.sem_inc(w_done, 2)
            with pool.Fori(0, 4) as i:
                for n in range(2):
                    pool.wait_ge(w_hi_done, i * 2 + (n + 1))
                    pool.tensor_tensor(w_lo[:, n, :, :], raw[:, n, :, :], w_hi[:, n, :, :].bitcast(F32),
                                       ALU.subtract).then_inc(w_done, 1)

        @block.vector
        def _(dve):
            own = Tally(dve, dve_own)
            for s, (c0, w_) in enumerate(PIECES if to_query else []):
                full = h_full[:, s % 2, :, 0:w_]
                hi, lo = k.hi[:, :, c0:c0 + w_], k.lo[:, :, c0:c0 + w_]
                if s == 2:
                    dve.wait_ge(h_split, 1)
                    modulate_sample(dve, own, k, *to_query, k.x_t[:, :, TP:T], full[:, :, LASTP:w_])
                dve.wait_ge(h_done, s + 1)
                own.do(dve.tensor_copy(hi, full))
                dve.tensor_tensor(lo, full, hi.bitcast(F32), ALU.subtract).then_inc(h_split, 1)
            for j in range(24):
                m, s = divmod(j, 3)
                c0, w_ = PIECES[s]
                dve.wait_ge(job_done, 6 + j + 1)
                if to_query:
                    dve.tensor_scalar(k.q_t[:, m, c0:c0 + w_], k.ps[j % BANKS][:, 0:w_], HD ** -0.5, None,
                                      ALU.mult).then_inc(bank_free, 1)
                else:
                    gated_add(dve, own, k, 1, 2, m, s, k.ps[j % BANKS], tmp, bank_free)

        @block.tensor
        def _(pe):
            pe.sem_inc(job_done, 6)
            pe.sem_inc(bank_free, BANKS)
            with pe.Fori(0, 4) as i:
                for j in range(6):
                    n, s = divmod(j, 3)
                    c0, w_ = PIECES[s]
                    if s == 0:
                        pe.wait_ge(w_done, i * 2 + (2 + n + 1))
                    if to_query:
                        pe.wait_ge(h_split, s + 1)
                    pe.wait_ge(bank_free, i * 6 + (j + 1))
                    for q in range(NC):
                        last = three(pe, k.ps[j % BANKS][:, 0:w_], w_hi[:, n, q, :], w_lo[:, n, q, :],
                                     k.hi[:, q, c0:c0 + w_], k.lo[:, q, c0:c0 + w_], q == 0, q == NC - 1)
                    last.then_inc(job_done, 1)


def attend_sample(nc, k, a):
    with ExitStack() as ctx:
        o = k.HH_AT
        k_t = k.at("sa_kt", [P, NC, 512], F32, o)
        k_pages = [k.at("sa_kpage0", [P, 4, D], F32, o + 16384), k.at("sa_kpage1", [P, 4, D], F32, o + 51712)]
        z_rows = k.at("sa_zrows", [P, 512], F32, o + 32768)
        t = k.at("sa_t", [P, 512], F32, o + 34816)
        spl = k.at("sa_sp", [P, 4, P], F32, o + 36864)
        sp_hi = k.at("sa_sphi", [P, 2, 4, P], F32R, o + 38912)
        sp_lo = k.at("sa_splo", [P, 2, 4, P], F32R, o + 43008)
        behind = k.at("sa_behind", [P, P], F32, o + 47104)
        behind_hi = k.at("sa_behindhi", [P, 2, P], F32R, o + 47616)
        q_tiles = k.at("sa_q", [P, NC, 32], F32, o + 49152)
        o_part = k.at("sa_op", [P, 4, HD], F32, o + 50176)
        o = k.WORK_AT
        v_page = k.at("sa_vpage", [P, 8, D], F32, o)
        k_new = k.at("sa_knew", [P, D], F32, o + 32768)
        v_new = k.at("sa_vnew", [P, D], F32, o + 36864)
        att = k.at("sa_a", [P, 2, 512], F32, o + 40960)
        behind_lo = k.at("sa_behindlo", [P, 2, P], F32R, o + 45056)
        pages2 = k.at("sa_pages2", [P, 2, P], F32, o + 46080)
        att_new = k.at("sa_anew", [P, DB, P], F32, o + 47104)
        sp_new = k.at("sa_spnew", [P, DB, P], F32, o + 51200)
        o_rows = k.at("sa_or", [P, DB, P], F32, o + 55296)
        att_b = k.at("sa_ab", [P, P], F32, o + 59392)
        o = k.HH_AT
        zn = k.at("sa_zn", [P, DB * P], F32, o)
        spn_hi = k.at("sa_spnhi", [P, DB * P], F32R, o + 4096)
        spn_lo = k.at("sa_spnlo", [P, DB * P], F32R, o + 8192)
        tn = k.at("sa_tn", [P, DB * P], F32, o + 12288)
        kn_t = k.at("sa_knt", [P, NC, P], F32, o + 32768)
        (zeroed, kn_in, vn_in, kn_turned, kn_kept, zn_part, zn_done, zn_kept, tn_own, tn_done, dve_new, spn_done, trin_done,
         an_done, k_turned, act_kept, dve_kept, z_done, z_kept, zt_done, act_own, t_done, s_done, sp_done, behind_done,
         pool_own, tri_done, a_done, ab_done, v_used, o_row, o_turned, dve_own, q_ready) = sems(
            ctx, nc, "sa", "zeroed", "kn_in", "vn_in", "kn_turned", "kn_kept", "zn_part", "zn_done", "zn_kept", "tn_own",
            "tn_done", "dve_new", "spn_done", "trin_done", "an_done", "k_turned", "act_kept", "dve_kept", "z_done",
            "z_kept", "zt_done", "act_own", "t_done", "s_done", "sp_done", "behind_done", "pool_own", "tri_done",
            "a_done", "ab_done", "v_used", "o_row", "o_turned", "dve_own", "q_ready")
        k_in = sems(ctx, nc, "sa", *[f"k_in{j}" for j in range(8)])
        v_in = sems(ctx, nc, "sa", *[f"v_in{j}" for j in range(8)])
        block = ctx.enter_context(nc.Block())
        UNITS = 8
        TURNS = 64
        Z, ZTS, OA = k.ps[3], [k.ps[4], k.ps[6]], k.ps[5]
        ZN = [k.ps[5], k.ps[6]]
        OT = [k.ps[6], k.ps[3]]
        TURN_BANKS = [k.ps[0], k.ps[1], k.ps[2], k.ps[7]]
        npages = a["cache_k"].shape[0]

        def by_head(ap):
            return ap.rearrange("p (b h q) -> p b h q", h=H, q=DS)

        @block.sync
        def _(sp):
            kc = a["cache_k"].rearrange("n p h d -> n p (h d)")
            vc = a["cache_v"].rearrange("n p h d -> n p (h d)")
            sp.wait_ge(zeroed, 2)
            sp.dma_start(k_new[0:TS, :], a["k_sample"].rearrange("b t h d -> (b t) (h d)")).then_inc(kn_in, 16)
            sp.dma_start(v_new[0:TS, :], a["v_sample"].rearrange("b t h d -> (b t) (h d)")).then_inc(vn_in, 16)
            with sp.Fori(0, DB) as b:
                page = {}
                for u in range(UNITS + 1):
                    for g in range(4 if u < UNITS else 0):
                        n = 4 * u + g
                        page[n] = sp.value_load(k.pages[0:1, bass.ds(b * PAGES + (PAGES - 1 - n), 1)],
                                                min_val=0, max_val=npages - 1)
                        sp.wait_ge(k_turned, b * TURNS + (2 * (n + 25) if n < 8 else 2 * (n - 7) + TURNS))
                        sp.dma_start(k_pages[u % 2][:, g, :], kc[bass.ds(page[n], 1), :, :].rearrange("n p d -> (n p) d")
                                     ).then_inc(k_in[n % 8], 16)
                    for g in range(4 if u else 0):
                        n = 4 * (u - 1) + g
                        sp.wait_ge(v_used, b * UNITS + (u + 6))
                        sp.dma_start(v_page[:, n % 8, :], vc[bass.ds(page[n], 1), :, :].rearrange("n p d -> (n p) d")
                                     ).then_inc(v_in[n % 8], 16)

        @block.gpsimd
        def _(pool):
            pool.memset(k_new[:, :], 0.0).then_inc(zeroed, 1)
            pool.memset(v_new[:, :], 0.0).then_inc(zeroed, 1)
            pool.memset(o_rows[:, :, :], 0.0).then_inc(zeroed, 1)
            own = Tally(pool, pool_own)
            OWN = 2 + 7 * 4
            pool.wait_ge(spn_done, 1)
            pool.wait_ge(an_done, 1)
            with pool.Fori(0, DB) as b:
                own.base, own.k = b * OWN, 0
                for u in range(UNITS):
                    hi, lo = behind_hi[:, u % 2, :], behind_lo[:, u % 2, :]
                    pool.wait_ge(s_done, b * UNITS + (u + 1))
                    pool.wait_ge(behind_done, b * UNITS + u)
                    if u == 0:
                        own.do(pool.tensor_tensor(behind[:, :], sp_new[:, bass.ds(b, 1), :].rearrange("p b n -> p (b n)"),
                                                  k.zeros[:, :], ALU.add))
                    else:
                        own.do(pool.tensor_tensor(pages2[:, :, :], spl[:, 0:2, :], spl[:, 2:4, :], ALU.add))
                        own.do(pool.tensor_tensor(pages2[:, 0, :], pages2[:, 0, :], pages2[:, 1, :], ALU.add))
                        own.do(pool.tensor_tensor(behind[:, :], behind[:, :], pages2[:, 0, :], ALU.add))
                    own.do(pool.tensor_tensor(hi, behind[:, :], k.zeros[:, :], ALU.add))
                    pool.tensor_tensor(lo, behind[:, :], hi.bitcast(F32), ALU.subtract).then_inc(behind_done, 1)
                    if u == 0:
                        pool.wait_ge(ab_done, b)
                        pool.tensor_tensor(att_b[:, :], att_new[:, bass.ds(b, 1), :].rearrange("p b n -> p (b n)"),
                                           k.zeros[:, :], ALU.add).then_inc(ab_done, 1)
                assert own.k == OWN, own.k

        def keep_turned(eng, copy, mine, b, u, kept, pages):
            for g in pages:
                for h in range(2):
                    job = 8 * u + 2 * g + h
                    if job % 2 != mine:
                        continue
                    eng.wait_ge(k_turned, b * TURNS + (TURNS + job + 1))
                    eng.wait_ge(z_done, b * UNITS + (u + 1))
                    copy(k_t[:, 4 * h:4 * h + 4, g * P:(g + 1) * P],
                         TURN_BANKS[job % 4][:, :].rearrange("p (c n) -> p c n", c=4)).then_inc(kept, 1)

        @block.scalar
        def _(act):
            act.preload_act_table_set("natural_log_exp_and_others")
            act.wait_ge(kn_turned, 1)
            act.activation(kn_t[:, 0:4, :], k.ps[0][:, :].rearrange("p (c n) -> p c n", c=4), ACT.Copy
                           ).then_inc(kn_kept, 1)
            act.wait_ge(zn_kept, 2)
            act.activation(tn[:, :], zn[:, :], ACT.Abs).then_inc(tn_own, 1)
            act.wait_ge(tn_own, 1)
            act.activation(tn[:, :], tn[:, :], ACT.Exp, scale=-1.0).then_inc(tn_own, 1)
            act.wait_ge(tn_own, 2)
            act.activation(tn[:, :], tn[:, :], ACT.Ln, bias=1.0).then_inc(tn_done, 1)
            act.wait_ge(zn_kept, 4)
            act.activation(att_new[:, :, :].rearrange("p b n -> p (b n)"), zn[:, :], ACT.Exp).then_inc(an_done, 1)
            act.wait_ge(an_done, 1)
            act.sem_inc(act_kept, 32)
            with act.Fori(0, DB) as b:
                def weights(u):
                    act.wait_ge(tri_done, b * UNITS + (u + 1))
                    act.activation(att[:, u % 2, :], ZTS[u % 2][:, :], ACT.Exp).then_inc(a_done, 1)

                def keep(u, pages):
                    keep_turned(act, lambda out, in_: act.activation(out, in_, ACT.Copy), 0, b, u, act_kept, pages)
                for u in range(UNITS):
                    keep(u, range(4))
                    if u:
                        weights(u - 1)
                    act.wait_ge(zt_done, b * UNITS + (u + 2))
                    act.wait_ge(s_done, b * UNITS + (u + 1))
                    act.activation(t[:, :], ZTS[u % 2][:, :], ACT.Abs).then_inc(act_own, 1)
                    act.wait_ge(act_own, b * (2 * UNITS) + (2 * u + 1))
                    act.activation(t[:, :], t[:, :], ACT.Exp, scale=-1.0).then_inc(act_own, 1)
                    act.wait_ge(act_own, b * (2 * UNITS) + (2 * u + 2))
                    act.activation(t[:, :], t[:, :], ACT.Ln, bias=1.0).then_inc(t_done, 1)
                weights(UNITS - 1)

        @block.vector
        def _(dve):
            new = Tally(dve, dve_new)
            dve.wait_ge(kn_turned, 2)
            dve.tensor_copy(kn_t[:, 4:8, :], k.ps[1][:, :].rearrange("p (c n) -> p c n", c=4)).then_inc(kn_kept, 1)
            bias = k.bias_all[:, :].unsqueeze(1).unsqueeze(3).to_broadcast([P, 4, H, DS])
            dve.wait_ge(zn_done, 1)
            for j in range(2):
                dve.tensor_tensor(by_head(zn[:, 512 * j:512 * j + 512]), by_head(ZN[j][:, :]), bias, ALU.add
                                  ).then_inc(zn_kept, 1)
            sp_flat = sp_new[:, :, :].rearrange("p b n -> p (b n)")
            dve.wait_ge(zn_kept, 2)
            dve.wait_ge(tn_done, 1)
            new.do(dve.scalar_tensor_tensor(sp_flat, zn[:, :], 0.0, tn[:, :], ALU.max, ALU.add))
            new.do(dve.tensor_copy(spn_hi[:, :], sp_flat))
            dve.tensor_tensor(spn_lo[:, :], sp_flat, spn_hi[:, :].bitcast(F32), ALU.subtract).then_inc(spn_done, 1)
            dve.wait_ge(trin_done, 1)
            for j in range(2):
                dve.tensor_tensor(by_head(zn[:, 512 * j:512 * j + 512]), by_head(ZN[j][:, :]), bias, ALU.add
                                  ).then_inc(zn_kept, 1)
            dve.wait_ge(an_done, 1)
            own = Tally(dve, dve_own)
            dve.sem_inc(dve_kept, 32)
            dve.sem_inc(z_kept, 1)
            dve.sem_inc(s_done, 1)
            dve.sem_inc(o_row, 1)
            own.do(dve.memset(q_tiles[:, :, :], 0.0))
            OWN = 3 + UNITS + 1
            with dve.Fori(0, DB) as b:
                own.base, own.k = b * OWN + 1, 0
                dve.wait_ge(z_done, b * UNITS + 1)
                for par in range(2):
                    for e in range(2):
                        half = slice(64 * par, 64 * par + 64)
                        c = 16 * e + 8 * par
                        ins = dve.tensor_copy(
                            q_tiles[half, :, :].rearrange("p (g e) c -> p g e c", e=2)[:, :, e, c:c + 8],
                            k.q_t[half, :, bass.ds(b * DS + TP, DS)].rearrange("p (g e) c -> p g e c", e=2)[:, :, e, :])
                        if par and e:
                            ins.then_inc(q_ready, 1)
                        else:
                            own.mark(ins)
                spu = spl[:, :, :].rearrange("p g c -> p (g c)")

                def keep(u, pages):
                    if u < UNITS:
                        keep_turned(dve, dve.tensor_copy, 1, b, u, dve_kept, pages)
                keep(0, range(4))
                for u in range(UNITS):
                    dve.wait_ge(z_done, b * UNITS + (u + 2))
                    dve.wait_ge(zt_done, b * UNITS + (u + 1))
                    dve.tensor_scalar(z_rows[:, :], Z[:, :], k.bias_row[:, 0:1], None, ALU.add).then_inc(z_kept, 1)
                    hi = sp_hi[:, u % 2, :, :].rearrange("p g c -> p (g c)")
                    lo = sp_lo[:, u % 2, :, :].rearrange("p g c -> p (g c)")
                    dve.wait_ge(t_done, b * UNITS + (u + 1))
                    dve.wait_ge(sp_done, b * UNITS + u)
                    dve.wait_ge(behind_done, b * UNITS + (u + 1 if u else 0))
                    dve.scalar_tensor_tensor(spu, ZTS[u % 2][:, :], 0.0, t[:, :], ALU.max, ALU.add).then_inc(s_done, 1)
                    keep(u + 1, [0])
                    dve.wait_ge(s_done, b * UNITS + (u + 2))
                    own.mark(dve.tensor_copy(hi, spu))
                    keep(u + 1, [1])
                    own.settle()
                    dve.tensor_tensor(lo, spu, hi.bitcast(F32), ALU.subtract).then_inc(sp_done, 1)
                    keep(u + 1, [2, 3])
                dve.wait_ge(v_used, b * UNITS + 2 * UNITS)
                dve.wait_ge(zeroed, 3)
                dve.wait_ge(o_row, b + 1)
                own.do(dve.tensor_tensor(o_part[:, :, :], OA[:, 0:4 * HD].rearrange("p (h d) -> p h d", h=4),
                                         over(k.block_of[:, :], HD), ALU.mult))
                dve.tensor_reduce(o_rows[:, bass.ds(b, 1), 0:HD].rearrange("p b d -> p (b d)"),
                                  o_part[:, :, :].rearrange("p h d -> p d h"), AX.X, ALU.add).then_inc(o_row, 1)
                assert own.k == OWN, own.k
            for j in range(2):
                dve.wait_ge(o_turned, j + 1)
                for par in range(2):
                    for c in range(NC):
                        dve.tensor_copy(
                            k.o_s[64 * par:64 * par + 64, c, 32 * j:32 * j + 32].rearrange("p (b q) -> p b q", q=DS),
                            OT[j][0:64, :].rearrange("p (b c r q) -> p b c r q", c=NC, r=2, q=DS)[:, :, c, par, :])

        @block.tensor
        def _(pe):
            pe.wait_ge(kn_in, 16)
            for j in range(2):
                for c in range(4):
                    last = pe.transpose(k.ps[j][:, c * P:(c + 1) * P], k_new[:, (4 * j + c) * P:(4 * j + c + 1) * P],
                                        k.ident[:, :])
                last.then_inc(kn_turned, 1)
            pe.wait_ge(kn_kept, 2)
            for step, (par, j) in enumerate(((0, 0), (1, 1), (0, 1), (1, 0))):
                if step == 2:
                    pe.wait_ge(zn_part, 2)
                half = slice(64 * par, 64 * par + 64)
                for c in range(NC):
                    last = pe.matmul(by_head(ZN[j][:, :])[:, :, 2 * c + par, :], kn_t[half, c, :],
                                     k.q_t[half, c, TP + 32 * j:TP + 32 * j + 32].rearrange("p (b q) -> p b q", q=DS),
                                     start=(step < 2 and c == 0), stop=False, skip_group_check=True)
                last.then_inc(zn_part, 1)
            pe.wait_ge(zn_part, 4)
            for j in range(2):
                last = pe.matmul(by_head(ZN[j][:, :]), k.ident_b[:, :],
                                 k.mask_new[:, 32 * j:32 * j + 32].rearrange("p (b q) -> p b q", q=DS).unsqueeze(2)
                                 .to_broadcast([P, 4, H, DS]), start=False, stop=False, skip_group_check=True)
            last.then_inc(zn_done, 1)
            pe.wait_ge(spn_done, 1)
            pe.wait_ge(zn_kept, 2)
            for j in range(2):
                for half in (spn_hi, spn_lo):
                    last = pe.matmul(ZN[j][:, :], k.neg_tri[:, :], half[:, 512 * j:512 * j + 512], start=False,
                                     stop=(half is spn_lo), skip_group_check=True)
            last.then_inc(trin_done, 1)
            pe.sem_inc(k_turned, TURNS)
            pe.sem_inc(z_done, 1)
            pe.sem_inc(zt_done, 1)
            pe.sem_inc(a_done, 1)
            pe.sem_inc(v_used, UNITS)
            with pe.Fori(0, DB) as b:
                def turn_keys(u):
                    for g in range(4):
                        for h in range(2):
                            job = 8 * u + 2 * g + h
                            if h == 0:
                                pe.wait_ge(k_in[4 * (u % 2) + g], b * 64 + 16 * (u // 2 + 1))
                            last_job = (job - 4) % TURNS
                            kept = act_kept if last_job % 2 == 0 else dve_kept
                            pe.wait_ge(kept, b * 32 + (last_job // 2 + 1 + (32 if job >= 4 else 0)))
                            for c in range(4):
                                last = pe.transpose(TURN_BANKS[job % 4][:, c * P:(c + 1) * P],
                                                    k_pages[u % 2][:, g, (4 * h + c) * P:(4 * h + c + 1) * P],
                                                    k.ident[:, :])
                            last.then_inc(k_turned, 1)

                def scores(u):
                    pe.wait_ge(act_kept, b * 32 + (32 + 4 * u + 4))
                    pe.wait_ge(dve_kept, b * 32 + (32 + 4 * u + 4))
                    pe.wait_ge(z_kept, b * UNITS + (u + 1))
                    if u == 0:
                        pe.wait_ge(q_ready, b + 1)
                    for e in range(2):
                        for q in range(4):
                            last = pe.matmul(Z[32 * q:32 * q + 32, :], q_tiles[:, 2 * q + e, :],
                                             k_t[:, 2 * q + e, :], start=(e == 0), stop=(e == 1),
                                             tile_position=(0, 32 * q), skip_group_check=True)
                    last.then_inc(z_done, 1)

                def turn_scores(u):
                    pe.wait_ge(z_kept, b * UNITS + (u + 2))
                    pe.wait_ge(a_done, b * UNITS + u)
                    for g in range(4):
                        last = pe.matmul(ZTS[u % 2][:, g * P:(g + 1) * P], z_rows[:, g * P:(g + 1) * P], k.ident[:, :],
                                         start=(g == 0), stop=False, is_transpose=True, skip_group_check=True)
                    last.then_inc(zt_done, 1)

                def subtract_sums(u):
                    pe.wait_ge(sp_done, b * UNITS + (u + 1))
                    pe.wait_ge(behind_done, b * UNITS + (u + 1))
                    terms = []
                    for half in (sp_hi, sp_lo):
                        terms.append((k.neg_tri, 0, half[:, u % 2, :, :]))
                        for g in range(3):
                            terms.append((k.neg_ones, g + 1, half[:, u % 2, g:g + 1, :]))
                    for half in (behind_hi, behind_lo):
                        terms.append((k.neg_ones, 0, half[:, u % 2:u % 2 + 1, :]))
                    for weight, g0, x in terms:
                        last = pe.matmul(ZTS[u % 2][:, g0 * P:].rearrange("p (g c) -> p g c", c=P), weight[:, :],
                                         x if x.shape[1] == 4 - g0 else x.to_broadcast([P, 4 - g0, P]), start=False,
                                         stop=x is terms[-1][2], skip_group_check=True)
                    last.then_inc(tri_done, 1)

                def add_values(weight, v, start, stop):
                    for q in range(4):
                        last = pe.matmul(OA[32 * q:32 * q + 32, 0:4 * HD], weight[:, 32 * q:32 * q + 32],
                                         v[:, 256 * q:256 * q + 256], start=start, stop=stop,
                                         tile_position=(0, 32 * q), skip_group_check=True)
                    return last

                def values(u):
                    if u == 0:
                        pe.wait_ge(ab_done, b + 1)
                        pe.wait_ge(vn_in, 16)
                        pe.wait_ge(o_row, b + 1)
                        add_values(att_b, v_new, True, False)
                    pe.wait_ge(a_done, b * UNITS + (u + 2))
                    for g in range(4):
                        slot = 4 * (u % 2) + g
                        pe.wait_ge(v_in[slot], b * 64 + 16 * (u // 2 + 1))
                        last = add_values(att[:, u % 2, g * P:(g + 1) * P], v_page[:, slot, :], False,
                                          u == UNITS - 1 and g == 3)
                    last.then_inc(v_used, 1)

                for u in range(UNITS):
                    turn_keys(u)
                    scores(u)
                    if u:
                        subtract_sums(u - 1)
                    turn_scores(u)
                    if u:
                        values(u - 1)
                subtract_sums(UNITS - 1)
                values(UNITS - 1)
            pe.wait_ge(o_row, DB + 1)
            for j in range(2):
                for b in range(4):
                    last = pe.transpose(OT[j][:, b * P:(b + 1) * P], o_rows[:, 4 * j + b, :], k.ident[:, :])
                last.then_inc(o_turned, 1)


def attend_prompt(nc, k, a):
    with ExitStack() as ctx:
        o = k.WORK_AT
        k_rows = k.at("pa_k", [P, 8, P], F32, o)
        v_rows = k.at("pa_v", [P, 2, 8, P], F32, o + 4096)
        k_t = k.at("pa_kt", [P, 2, TP], F32, o + 12288)
        q_s = k.at("pa_q", [P, 2, 512], F32, o + 20480)
        t = k.at("pa_t", [P, 2, 512], F32, o + 24576)
        spl = k.at("pa_sp", [P, 2, 512], F32, o + 28672)
        sp_hi = k.at("pa_sphi", [P, 4, 512], F32R, o + 32768)
        sp_lo = k.at("pa_splo", [P, 4, 512], F32R, o + 40960)
        att = k.at("pa_a", [P, 3, 512], F32, o + 49152)
        behind = k.at("pa_behind", [P, 2, 2, 512], F32, o + 55296)
        bias = k.at("pa_bias", [P, 4], F32, o + 63488)
        (z_done, act_own, t_done, s_done, sp_done, behind_done, tri_done, a_done, pv_done, dve_own, k_turned,
         k_kept, q_ready, o_kept, k_in) = sems(ctx, nc, "pa", "z_done", "act_own", "t_done", "s_done", "sp_done", "behind_done", "tri_done",
                        "a_done", "pv_done", "dve_own", "k_turned", "k_kept", "q_ready", "o_kept", "k_in")
        v_in = sems(ctx, nc, "pa", "v_in0", "v_in1")
        block = ctx.enter_context(nc.Block())
        NT = 48
        Z = [k.ps[b] for b in (0, 1, 2, 3, 6, 7)]
        TURN_NEXT = (18, 20)
        Q_FOR = {0: (0, 0), 8: (0, 1), 24: (1, 0), 32: (1, 1)}

        class Tile:
            pass
        tiles = []
        for pp in range(2):
            for half in range(2):
                last_j = 4 * half + 3
                for n, j in enumerate(range(last_j, -1, -1)):
                    for head in range(2):
                        x = Tile()
                        x.pp, x.half, x.j, x.head, x.n = pp, half, j, head, n
                        x.q0 = max(P * j, 512 * half)
                        x.lo = x.q0 - 512 * half
                        x.w = 512 - x.lo
                        x.diag = P * j >= 512 * half
                        x.first, x.last = n == 0, j == 0
                        x.carry = P if x.diag else 0
                        x.acc = k.ps[4 + (2 * pp + half) % 2]
                        x.slot = len(tiles) // 2 % 2
                        tiles.append(x)
        ends = {i: x for i, x in enumerate(tiles) if x.last and x.head == 1}
        steps = [0 if x.last else 1 if x.first or not x.diag else 2 for x in tiles]
        behind_of = [sum(steps[:n + 1]) for n in range(NT)]
        BEHIND = behind_of[-1]

        @block.sync
        def _(sp):
            kp = a["k_prompt"][0].rearrange("(j p) h d -> p j (h d)", p=P)
            vp = a["v_prompt"][0].rearrange("(j p) h d -> p j (h d)", p=P)
            with sp.Fori(0, 4) as i:
                for pp in range(2):
                    cols = bass.ds((i * 2 + pp) * P, P)
                    sp.wait_ge(k_turned, i * 4 + 2 * pp)
                    sp.dma_start(k_rows[:, :, :], kp[:, :, cols]).then_inc(k_in, 16)
                    sp.wait_ge(pv_done, i * NT + 24 * (pp + 1))
                    sp.dma_start(v_rows[:, pp, :, :], vp[:, :, cols]).then_inc(v_in[pp], 16)

        @block.scalar
        def _(act):
            act.preload_act_table_set("natural_log_exp_and_others")
            with act.Fori(0, 4) as i:
                def keep_keys(pp, h, bank):
                    act.wait_ge(k_turned, i * 4 + (2 * pp + h + 1))
                    act.wait_ge(z_done, i * NT + 24 * (pp + 1))
                    act.activation(k_t[:, pp, 512 * h:512 * h + 512], k.ps[bank][:, :], ACT.Copy).then_inc(k_kept, 1)
                for h in range(2):
                    keep_keys(0, h, 6 + h)
                act.wait_ge(q_ready, i * 4 + 2)
                for n in range(NT + 3):
                    if n in TURN_NEXT:
                        keep_keys(1, TURN_NEXT.index(n), 4)
                    if n < NT:
                        x = tiles[n]
                        tt, zz = t[:, n % 2, 0:x.w], Z[n % 6][:, 0:x.w]
                        b = bias[:, 2 * x.pp + x.head:2 * x.pp + x.head + 1]
                        act.wait_ge(z_done, i * NT + (NT + n + 1))
                        act.wait_ge(s_done, i * NT + (n + 1))
                        act.activation(tt, zz, ACT.Abs, bias=b).then_inc(act_own, 1)
                        act.wait_ge(act_own, i * (2 * NT) + (2 * n + 1))
                        act.activation(tt, tt, ACT.Exp, scale=-1.0).then_inc(act_own, 1)
                    m = n - 3
                    if m >= 0:
                        x = tiles[m]
                        act.wait_ge(tri_done, i * NT + (4 + m + 1))
                        act.wait_ge(pv_done, i * NT + (NT + m - 2))
                        act.activation(att[:, m % 3, 0:x.w], Z[m % 6][:, 0:x.w], ACT.Exp,
                                       bias=bias[:, 2 * x.pp + x.head:2 * x.pp + x.head + 1]).then_inc(a_done, 1)
                    if n < NT:
                        act.wait_ge(act_own, i * (2 * NT) + (2 * n + 2))
                        act.activation(tt, tt, ACT.Ln, bias=1.0).then_inc(t_done, 1)

        @block.gpsimd
        def _(pool):
            with pool.Fori(0, 4) as i:
                for n, x in enumerate(tiles):
                    if x.last:
                        continue
                    s = spl[:, n % 2, 0:x.w]
                    b_in, b_out = behind[:, x.head, x.slot, :], behind[:, x.head, (x.slot + 1) % 2, :]
                    new = x.w if x.first else x.carry
                    pool.wait_ge(s_done, i * NT + (2 + n + 1))
                    pool.wait_ge(tri_done, i * NT + (n + 3))
                    pool.wait_ge(behind_done, i * BEHIND + (behind_of[n - 2] if n >= 2 else 0))
                    if new:
                        pool.tensor_tensor(b_out[:, x.lo:x.lo + new], s[:, 0:new], k.zeros[:, 0:new], ALU.add
                                           ).then_inc(behind_done, 1)
                    if new < x.w:
                        pool.tensor_tensor(b_out[:, x.lo + new:512], b_in[:, x.lo + new:512], s[:, new:x.w], ALU.add
                                           ).then_inc(behind_done, 1)

        @block.vector
        def _(dve):
            own = Tally(dve, dve_own)
            dve.sem_inc(s_done, 2)
            dve.sem_inc(o_kept, 2)
            own.do(dve.tensor_copy(k.hi[:, :, TP:T], k.o_s[:, :, :]))
            own.do(dve.tensor_tensor(k.lo[:, :, TP:T], k.o_s[:, :, :], k.hi[:, :, TP:T].bitcast(F32), ALU.subtract))
            before = own.k
            OWN = 1 + 2 * NT + 4
            with dve.Fori(0, 4) as i:
                own.base, own.k = i * OWN + before, 0
                dve.wait_ge(z_done, i * NT + NT)
                dve.wait_ge(a_done, i * NT + 6)

                def copy_q(pp, half):
                    cols = slice(512 * half, 512 * half + 512)
                    dve.tensor_copy(q_s[:, half, :], k.q_t[:, bass.ds(i * 2 + pp, 1), cols].rearrange("p c n -> p (c n)")
                                    ).then_inc(q_ready, 1)

                copy_q(0, 0)
                own.do(dve.tensor_copy(bias[:, :], k.bias_all[:, bass.ds(i * 4, 4)]))
                copy_q(0, 1)

                def keep_output(x):
                    dve.wait_ge(pv_done, i * NT + (NT + tiles.index(x) + 1))
                    cols = slice(512 * x.half, 512 * x.half + 512)
                    hi = k.hi[:, bass.ds(i * 2 + x.pp, 1), cols].rearrange("p c n -> p (c n)")
                    lo = k.lo[:, bass.ds(i * 2 + x.pp, 1), cols].rearrange("p c n -> p (c n)")
                    own.do(dve.tensor_copy(hi, x.acc[:, :]))
                    dve.tensor_tensor(lo, x.acc[:, :], hi.bitcast(F32), ALU.subtract).then_inc(o_kept, 1)

                for n in range(NT + 6):
                    if n in (10, 26):
                        dve.wait_ge(z_done, i * NT + (NT + n - 2))
                        copy_q(1, int(n == 26))
                    m = n - 1
                    if 0 <= m < NT:
                        y = tiles[m]
                        s = spl[:, m % 2, 0:y.w]
                        dve.wait_ge(t_done, i * NT + (m + 1))
                        own.settle()
                        dve.tensor_tensor(s, s, t[:, m % 2, 0:y.w], ALU.add).then_inc(s_done, 1)
                    if n < NT:
                        x = tiles[n]
                        dve.wait_ge(act_own, i * (2 * NT) + (2 * n + 1))
                        dve.wait_ge(sp_done, i * NT + max(n - 1, 0))
                        dve.wait_ge(behind_done, i * BEHIND + (behind_of[n - 2] if n >= 2 else 0))
                        own.mark(dve.tensor_scalar(spl[:, n % 2, 0:x.w], Z[n % 6][:, 0:x.w],
                                                   bias[:, 2 * x.pp + x.head:2 * x.pp + x.head + 1], 0.0,
                                                   ALU.add, ALU.max))
                    if 0 <= m < NT:
                        hi, lo = sp_hi[:, m % 4, 0:y.w], sp_lo[:, m % 4, 0:y.w]
                        dve.wait_ge(s_done, i * NT + (2 + m + 1))
                        dve.wait_ge(tri_done, i * NT + (m + 1))
                        own.do(dve.tensor_copy(hi, s))
                        dve.tensor_tensor(lo, s, hi.bitcast(F32), ALU.subtract).then_inc(sp_done, 1)
                    if n - 6 in ends:
                        keep_output(ends[n - 6])
                assert own.k == OWN, (own.k, OWN)

        @block.tensor
        def _(pe):
            pe.sem_inc(pv_done, NT)
            pe.sem_inc(z_done, NT)
            pe.sem_inc(tri_done, 4)
            pe.sem_inc(a_done, 6)
            with pe.Fori(0, 4) as i:
                def turn_keys(h, bank):
                    for c in range(4):
                        last = pe.transpose(k.ps[bank][:, c * P:(c + 1) * P], k_rows[:, 4 * h + c, :], k.ident[:, :])
                    last.then_inc(k_turned, 1)
                pe.wait_ge(k_in, i * 32 + 16)
                pe.wait_ge(a_done, i * NT + 6)
                for h in range(2):
                    turn_keys(h, 6 + h)
                pe.wait_ge(k_kept, i * 4 + 2)
                for n in range(NT + 4):
                    if n in TURN_NEXT:
                        h = TURN_NEXT.index(n)
                        pe.wait_ge(k_in, i * 32 + 32)
                        pe.wait_ge(o_kept, i * 4 + 3)
                        pe.wait_ge(k_kept, i * 4 + (2 + h))
                        turn_keys(h, 4)
                    if n == 24:
                        pe.wait_ge(k_kept, i * 4 + 4)
                    if n in Q_FOR:
                        pe.wait_ge(q_ready, i * 4 + (list(Q_FOR).index(n) + 1))
                    if n < NT:
                        x = tiles[n]
                        rows = slice(64 * x.head, 64 * x.head + 64)
                        z = Z[n % 6]
                        pe.wait_ge(a_done, i * NT + (n + 1))
                        last = pe.matmul(z[:, 0:x.w], k_t[rows, x.pp, P * x.j:P * x.j + P],
                                         q_s[rows, x.half, x.lo:512], start=True, stop=False,
                                         skip_group_check=True)
                        if x.diag:
                            last = pe.matmul(z[:, 0:P], k.ident_b[:, :], k.mask_diag[:, :], start=False, stop=False,
                                             skip_group_check=True)
                        last.then_inc(z_done, 1)
                    if 0 <= n - 3 < NT:
                        m = n - 3
                        x = tiles[m]
                        z = Z[m % 6]
                        pe.wait_ge(sp_done, i * NT + (m + 1))
                        pe.matmul(z[:, 0:x.w], k.neg_tri[:, :], sp_hi[:, m % 4, 0:x.w], start=False, stop=False,
                                  skip_group_check=True)
                        last = pe.matmul(z[:, 0:x.w], k.neg_tri[:, :], sp_lo[:, m % 4, 0:x.w], start=False, stop=x.first,
                                         skip_group_check=True)
                        if not x.first:
                            pe.wait_ge(behind_done, i * BEHIND + behind_of[m - 2])
                            last = pe.matmul(z[:, x.carry:x.w], k.neg_ones[:, :].bitcast(F32),
                                             behind[:, x.head, x.slot, x.lo + x.carry:512], start=False, stop=True,
                                             skip_group_check=True)
                        last.then_inc(tri_done, 1)
                    if 0 <= n - 4:
                        m = n - 4
                        x = tiles[m]
                        pe.wait_ge(a_done, i * NT + (6 + m + 1))
                        if m % 24 == 0:
                            pe.wait_ge(v_in[x.pp], i * 16 + 16)
                        if x.first and x.head == 0:
                            pe.wait_ge(o_kept, i * 4 + (2 * x.pp + x.half + 1))
                        pe.matmul(x.acc[64 * x.head:64 * x.head + 64, x.lo:512],
                                  v_rows[:, x.pp, x.j, 64 * x.head:64 * x.head + 64], att[:, m % 3, 0:x.w],
                                  start=x.first, stop=x.last, skip_group_check=True).then_inc(pv_done, 1)


def store_y(nc, k, a):
    with ExitStack() as ctx:
        y_rows = k.at("y_rows", [P, 9, D], F32, k.HH_AT)
        turned, act_kept, dve_kept, stored = sems(ctx, nc, "y", "turned", "act_kept", "dve_kept", "stored")
        block = ctx.enter_context(nc.Block())
        JOBS = 18

        def keep(eng, copy, mine, kept):
            for j in range(mine, JOBS, 2):
                t, half = divmod(j, 2)
                rows = P if t < 8 else TS
                eng.wait_ge(turned, j + 1)
                copy(y_rows[0:rows, t, 512 * half:512 * half + 512], k.ps[j % 8][0:rows, :]).then_inc(kept, 1)

        @block.tensor
        def _(pe):
            for j in range(JOBS):
                t, half = divmod(j, 2)
                rows = P if t < 8 else TS
                if j >= 8:
                    pe.wait_ge(dve_kept if j % 2 else act_kept, (j - 8) // 2 + 1)
                for c in range(4):
                    last = pe.transpose(k.ps[j % 8][0:rows, c * P:(c + 1) * P],
                                        k.x_t[:, 4 * half + c, t * P:t * P + rows], k.ident[:, :])
                last.then_inc(turned, 1)

        @block.scalar
        def _(act):
            keep(act, lambda out, in_: act.activation(out, in_, ACT.Copy), 0, act_kept)

        @block.vector
        def _(dve):
            keep(dve, dve.tensor_copy, 1, dve_kept)

        @block.sync
        def _(sp):
            for t in range(9):
                sp.wait_ge(act_kept, t + 1)
                sp.wait_ge(dve_kept, t + 1)
                dst = a["y_prompt"][0, t * P:(t + 1) * P, :] if t < 8 else a["y_sample"].rearrange("b t d -> (b t) d")
                sp.dma_start(dst, y_rows[0:P if t < 8 else TS, t, :]).then_inc(stored, 16)
            sp.wait_ge(stored, 9 * 16)


def build(nc, a):
    k = Kernel()
    base = -(-nc.sbuf_base // 64) * 64
    end = nc.sbuf_usable_end
    X_BYTES = NC * T * 4

    placed = {}

    def at(name, shape, dtype, offset):
        if name not in placed:
            placed[name] = nc.alloc_sbuf_tensor_at(name, shape, dtype, offset=offset)
        return placed[name]
    k.at = at
    k.HH_AT = base + X_BYTES
    k.F_AT = k.HH_AT + 2 * X_BYTES
    k.WORK_AT = k.F_AT + X_BYTES
    WORK = 65280
    k.x_t = at("x_t", [P, NC, T], F32, base)
    k.hi = at("hi", [P, NC, T], F32R, k.HH_AT)
    k.lo = at("lo", [P, NC, T], F32R, k.HH_AT + X_BYTES)
    k.q_t = at("q_t", [P, NC, T], F32, k.F_AT)
    place = [k.WORK_AT + WORK]

    def const(name, shape, dtype):
        n = 1
        for x in shape[1:]:
            n *= x
        n *= {F32: 4, F32R: 4, I32: 4, BF16: 2}[dtype]
        got = at(name, shape, dtype, place[0])
        place[0] += -(-n // 64) * 64
        assert place[0] <= end, (name, place[0], end)
        return got
    k.ident = const("ident", [P, P], F32)
    k.mean_of = const("mean_of", [P, P], F32)
    k.zeros = const("zeros", [P, P], F32)
    k.neg_ones = const("neg_ones", [P, P], F32R)
    k.neg_tri = const("neg_tri", [P, P], F32R)
    k.ident_b = const("ident_b", [P, P], BF16)
    k.mask_diag = const("mask_diag", [P, P], BF16)
    k.mask_new = const("mask_new", [P, TS], BF16)
    k.mod = [const(f"mod{i}", [P, 48, 9], F32) for i in range(2)]
    k.vec_t = const("vec_t", [P, 168], F32)
    k.bias_all = const("bias_all", [P, H], F32)
    k.head_of = const("head_of", [P, H], F32)
    k.block_of = const("block_of", [P, 4], F32)
    k.bias_row = const("bias_row", [P, 1], F32)
    k.inv_seen = const("inv_seen", [P, 16], F32)
    k.c_t = at("c_t", [P, NC, 32], F32, k.F_AT + 12288)
    k.scratch = at("scratch", [P, P], F32, k.F_AT + 20480)
    k.o_s = at("o_s", [P, NC, TS], F32, k.WORK_AT + WORK - 64 - 1472 - 2048 + 1472)
    k.pages = at("pages", [1, DB * PAGES], I32, k.WORK_AT + WORK - 64 - 2048 - 1088)
    v = k.vec_t
    k.b_ada = [v[:, 0:48], v[:, 48:96]]
    k.ln_g = [[v[:, 96 + 16 * l + 8 * w:104 + 16 * l + 8 * w] for w in range(2)] for l in range(2)]
    k.ln_b = [[v[:, 128 + 16 * l + 8 * w:136 + 16 * l + 8 * w] for w in range(2)] for l in range(2)]
    k.pool_scale = v[:, 160:168]
    k.ps = [nc.alloc_psum_tensor(f"bank{i}", [P, 512], F32) for i in range(8)]

    steps = [
        lambda: setup(nc, k, a),
        lambda: pool_mixer(nc, k, a),
        lambda: norm(nc, k, "n00", 0, 0, (0, 4, 3)),
        lambda: mlp(nc, k, "m0", 0, a["w_up"], a["w_down"]),
        lambda: norm(nc, k, "n01", 0, 1, "x"),
        lambda: keys_values(nc, k, a),
        lambda: project(nc, k, "q", a["w_q"], (1, 1, 0)),
        lambda: attend_sample(nc, k, a),
        lambda: attend_prompt(nc, k, a),
        lambda: project(nc, k, "wo", a["w_o"], None),
        lambda: norm(nc, k, "n10", 1, 0, (1, 4, 3)),
        lambda: mlp(nc, k, "m1", 1, a["w_up"], a["w_down"]),
        lambda: norm(nc, k, "n11", 1, 1, None),
        lambda: store_y(nc, k, a),
    ]
    for step in steps:
        step()


INS = ["x_prompt", "x_sample", "cache_k", "cache_v", "state_pool", "page_table", "c_prompt", "c_sample", "w_ada",
       "b_ada", "ln_g", "ln_b", "w_pool", "pool_scale", "w_up", "w_down", "w_kv", "w_q", "w_o", "b_break"]
OUTS = {
    "y_prompt": (1, TP, D), "y_sample": (DB, DS, D), "k_prompt": (1, TP, H, HD), "v_prompt": (1, TP, H, HD),
    "pool_prompt": (1, 1, HIST, D), "k_sample": (DB, DS, H, HD), "v_sample": (DB, DS, H, HD),
    "pool_sample": (1, DB, HIST, D),
}


def kernel(**inputs):
    import numpy as np
    import concourse.bacc as bacc
    from concourse.bass_utils import run_bass_kernel_spmd

    nc = bacc.Bacc("TRN2", target_bir_lowering=False, num_devices=1)
    arrays, aps = {}, {}
    for name in INS:
        x = np.ascontiguousarray(inputs[name])
        arrays[f"in_{name}"] = x
        aps[name] = nc.dram_tensor(f"in_{name}", x.shape, mybir.dt.from_np(x.dtype), kind="ExternalInput").ap()
    for name, shape in OUTS.items():
        aps[name] = nc.dram_tensor(f"out_{name}", shape, F32, kind="ExternalOutput").ap()
    build(nc, aps)
    r = run_bass_kernel_spmd(nc, [arrays], core_ids=[0])
    return tuple(r.results[0][f"out_{name}"] for name in OUTS)
```
